# Optimizing a Trainium2 kernel written in Bass

```python
import math
import jax, jax.numpy as jnp
from jax import lax
import numpy as np

D_MODEL = 2048
BATCH = 1
SEQ = 256
DEPTH = 1

DN_HEADS = 16
DN_DK = 128
DN_DV = 128
DN_CONV = 4
DN_CHUNK = 64
DN_QK = DN_HEADS * DN_DK
DN_V = DN_HEADS * DN_DV
DA_HEADS = 16
DA_HEAD_DIM = 64
DA_V_DIM = 2 * DA_HEAD_DIM
DA_QK = DA_HEADS * 2 * DA_HEAD_DIM
DA_V = DA_HEADS * DA_V_DIM
Q_BLOCK = 128
D_FF = -(-8 * D_MODEL // (3 * 256)) * 256
DEEPNORM_ALPHA = (2 * DEPTH) ** 0.25
DEEPNORM_BETA = (8 * DEPTH) ** -0.25
LN_EPS = 1e-5
RMS_EPS = 1e-6
IN_SIZES = (DN_QK, DN_QK, DN_V, DN_V, DN_HEADS, DN_HEADS, DA_QK, DA_QK, DA_V, D_MODEL, D_MODEL)
D_IN = sum(IN_SIZES)

kernel_name = 'hybrid_gdn_diffattn_alibi_deepnorm'

def _partition_bounds():
    bounds = [0]
    for s in IN_SIZES:
        bounds.append(bounds[-1] + s)
    return bounds

def _alibi_slopes(n_heads):
    h = jnp.arange(1, n_heads + 1, dtype=jnp.float32)
    return jnp.exp2(-8.0 * h / n_heads)

def layer_norm(x, g, b):
    xf = x.astype(jnp.float32)
    mu = jnp.mean(xf, axis=-1, keepdims=True)
    xc = xf - mu
    var = jnp.mean(xc * xc, axis=-1, keepdims=True)
    return (xc * lax.rsqrt(var + LN_EPS) * g + b).astype(x.dtype)

def rms_norm(x, w):
    xf = x.astype(jnp.float32)
    return xf * lax.rsqrt(jnp.mean(xf * xf, axis=-1, keepdims=True) + RMS_EPS) * w

def l2_normalize(x):
    xf = x.astype(jnp.float32)
    return xf * lax.rsqrt(jnp.sum(xf * xf, axis=-1, keepdims=True) + RMS_EPS)

def causal_depthwise_conv(x, w):
    K, C = w.shape
    return lax.conv_general_dilated(
        x, w[:, None, :].astype(x.dtype), window_strides=(1,), padding=[(K - 1, 0)],
        dimension_numbers=('NWC', 'WIO', 'NWC'), feature_group_count=C)

def chunk_gated_delta_rule(q, k, v, g, beta):
    B, H, L, dk = q.shape
    dv = v.shape[-1]
    C = DN_CHUNK
    N = L // C
    f32 = jnp.float32
    q = q.astype(f32).reshape(B, H, N, C, dk)
    k = k.astype(f32).reshape(B, H, N, C, dk)
    v = v.astype(f32).reshape(B, H, N, C, dv)
    g = jnp.cumsum(g.astype(f32).reshape(B, H, N, C), axis=-1)
    beta = beta.astype(f32).reshape(B, H, N, C, 1)
    causal = jnp.tril(jnp.ones((C, C), dtype=bool))
    strict = jnp.tril(jnp.ones((C, C), dtype=bool), -1)
    decay = jnp.exp(jnp.where(causal, g[..., :, None] - g[..., None, :], -jnp.inf))
    k_beta = k * beta
    a_mat = jnp.where(strict, jnp.einsum('bhncd,bhnsd->bhncs', k_beta, k) * decay, 0.0)
    rhs = jnp.concatenate([v * beta, k_beta * jnp.exp(g)[..., None]], axis=-1)
    sol = lax.linalg.triangular_solve(a_mat + jnp.eye(C, dtype=f32), rhs, left_side=True,
                                      lower=True, unit_diagonal=True)
    u, w = sol[..., :dv], sol[..., dv:]
    qk = jnp.einsum('bhncd,bhnsd->bhncs', q, k) * decay
    q_dec = q * jnp.exp(g)[..., None]
    k_tail = k * jnp.exp(g[..., -1:] - g)[..., None]
    g_tot = jnp.exp(g[..., -1])

    def step(S, xs):
        qk_c, qd_c, u_c, w_c, kt_c, gt_c = xs
        v_new = u_c - jnp.einsum('bhcd,bhde->bhce', w_c, S)
        o_c = jnp.einsum('bhcd,bhde->bhce', qd_c, S) + jnp.einsum('bhcs,bhse->bhce', qk_c, v_new)
        S = S * gt_c[..., None, None] + jnp.einsum('bhcd,bhce->bhde', kt_c, v_new)
        return S, o_c

    xs = (jnp.moveaxis(qk, 2, 0), jnp.moveaxis(q_dec, 2, 0), jnp.moveaxis(u, 2, 0),
          jnp.moveaxis(w, 2, 0), jnp.moveaxis(k_tail, 2, 0), jnp.moveaxis(g_tot, 2, 0))
    S0 = jnp.zeros((B, H, dk, dv), f32)
    _, o = lax.scan(step, S0, xs)
    return jnp.moveaxis(o, 0, 2).reshape(B, H, L, dv)

def gated_deltanet(q, k, v, z, beta_logit, a_logit, conv_w, a_log, dt_bias, norm_w):
    B, L, _ = q.shape
    qkv = jax.nn.silu(causal_depthwise_conv(jnp.concatenate([q, k, v], axis=-1), conv_w))
    q, k, v = jnp.split(qkv, [DN_QK, 2 * DN_QK], axis=-1)
    q = l2_normalize(q.reshape(B, L, DN_HEADS, DN_DK)) * (DN_DK ** -0.5)
    k = l2_normalize(k.reshape(B, L, DN_HEADS, DN_DK))
    v = v.reshape(B, L, DN_HEADS, DN_DV)
    beta = jax.nn.sigmoid(beta_logit.astype(jnp.float32))
    g = -jnp.exp(a_log) * jax.nn.softplus(a_logit.astype(jnp.float32) + dt_bias)
    o = chunk_gated_delta_rule(q.transpose(0, 2, 1, 3), k.transpose(0, 2, 1, 3), v.transpose(0, 2, 1, 3),
                               g.transpose(0, 2, 1), beta.transpose(0, 2, 1))
    o = o.transpose(0, 2, 1, 3)
    o = rms_norm(o, norm_w) * jax.nn.silu(z.reshape(B, L, DN_HEADS, DN_DV).astype(jnp.float32))
    return o.reshape(B, L, DN_V).astype(z.dtype)

def diff_attention(q, k, v, lam_params, norm_w, layer_idx):
    B, L, _ = q.shape
    q = q.reshape(B, L, DA_HEADS, 2, DA_HEAD_DIM).transpose(0, 2, 3, 1, 4)
    k = k.reshape(B, L, DA_HEADS, 2, DA_HEAD_DIM).transpose(0, 2, 3, 1, 4)
    v = v.reshape(B, L, DA_HEADS, DA_V_DIM).transpose(0, 2, 1, 3)
    lambda_init = 0.8 - 0.6 * math.exp(-0.3 * layer_idx)
    lp = lam_params.astype(jnp.float32)
    lam = jnp.exp(jnp.sum(lp[0] * lp[1])) - jnp.exp(jnp.sum(lp[2] * lp[3])) + lambda_init
    slopes = _alibi_slopes(DA_HEADS)
    scale = DA_HEAD_DIM ** -0.5
    outs = []
    for blk in range(L // Q_BLOCK):
        start, end = blk * Q_BLOCK, (blk + 1) * Q_BLOCK
        qb = q[:, :, :, start:end]
        kb = k[:, :, :, :end]
        vb = v[:, :, :end]
        dist = (jnp.arange(start, end)[:, None] - jnp.arange(end)[None, :]).astype(jnp.float32)
        bias = jnp.where(dist >= 0, -slopes[:, None, None] * dist, -jnp.inf)
        s = jnp.einsum('bhmqd,bhmkd->bhmqk', qb, kb).astype(jnp.float32) * scale + bias[None, :, None]
        p = jax.nn.softmax(s, axis=-1)
        p_diff = p[:, :, 0] - lam * p[:, :, 1]
        outs.append(jnp.einsum('bhqk,bhkd->bhqd', p_diff, vb.astype(jnp.float32)))
    o = jnp.concatenate(outs, axis=2)
    o = rms_norm(o, norm_w) * (1.0 - lambda_init)
    return o.transpose(0, 2, 1, 3).reshape(B, L, DA_V).astype(v.dtype)

def setup_inputs(seed: int = 0) -> dict:
    key = jax.random.key(seed)
    ks = jax.random.split(key, 16)
    f32 = jnp.float32
    bounds = _partition_bounds()

    def dense(k, shape, fan_in, gain=1.0):
        return jax.random.normal(k, shape, f32) * (gain * fan_in ** -0.5)

    col_scale = np.ones((D_IN,), np.float32)
    col_scale[bounds[2]:bounds[3]] = DEEPNORM_BETA
    col_scale[bounds[8]:bounds[9]] = DEEPNORM_BETA

    x = jax.random.normal(ks[0], (BATCH, SEQ, D_MODEL), f32)
    w_in = dense(ks[1], (DEPTH, D_MODEL, D_IN), D_MODEL) * jnp.asarray(col_scale)
    conv_w = dense(ks[2], (DEPTH, DN_CONV, 2 * DN_QK + DN_V), DN_CONV)
    a_log = jnp.log(jax.random.uniform(ks[3], (DEPTH, DN_HEADS), f32, 1.0, 16.0))
    dt = jnp.exp(jax.random.uniform(ks[4], (DEPTH, DN_HEADS), f32, math.log(1e-3), math.log(1e-1)))
    dt_bias = dt + jnp.log(-jnp.expm1(-dt))
    dn_norm_w = 1.0 + 0.02 * jax.random.normal(ks[5], (DEPTH, DN_DV), f32)
    da_lambda = 0.1 * jax.random.normal(ks[6], (DEPTH, 4, DA_HEAD_DIM), f32)
    da_norm_w = 1.0 + 0.02 * jax.random.normal(ks[7], (DEPTH, DA_V_DIM), f32)
    w_branch_a = dense(ks[8], (DEPTH, DN_V, D_MODEL), DN_V, DEEPNORM_BETA)
    w_branch_b = dense(ks[9], (DEPTH, DA_V, D_MODEL), DA_V, DEEPNORM_BETA)
    w_out = dense(ks[10], (DEPTH, D_MODEL, D_MODEL), D_MODEL, DEEPNORM_BETA)
    ln_g = 1.0 + 0.02 * jax.random.normal(ks[11], (DEPTH, 2, D_MODEL), f32)
    ln_b = 0.02 * jax.random.normal(ks[12], (DEPTH, 2, D_MODEL), f32)
    w_gate = dense(ks[13], (DEPTH, D_MODEL, D_FF), D_MODEL, DEEPNORM_BETA)
    w_up = dense(ks[14], (DEPTH, D_MODEL, D_FF), D_MODEL, DEEPNORM_BETA)
    w_down = dense(ks[15], (DEPTH, D_FF, D_MODEL), D_FF, DEEPNORM_BETA)
    return {'x': x, 'w_in': w_in, 'conv_w': conv_w, 'a_log': a_log, 'dt_bias': dt_bias,
            'dn_norm_w': dn_norm_w, 'da_lambda': da_lambda, 'da_norm_w': da_norm_w,
            'w_branch_a': w_branch_a, 'w_branch_b': w_branch_b, 'w_out': w_out,
            'ln_g': ln_g, 'ln_b': ln_b, 'w_gate': w_gate, 'w_up': w_up, 'w_down': w_down}

def reference(x, w_in, conv_w, a_log, dt_bias, dn_norm_w, da_lambda, da_norm_w,
              w_branch_a, w_branch_b, w_out, ln_g, ln_b, w_gate, w_up, w_down):
    split_at = _partition_bounds()[1:-1]
    for l in range(DEPTH):
        h = x @ w_in[l]
        dq, dk, dv, dz, db, da, aq, ak, av, ga, gb = jnp.split(h, split_at, axis=-1)
        o_a = gated_deltanet(dq, dk, dv, dz, db, da, conv_w[l], a_log[l], dt_bias[l], dn_norm_w[l])
        o_b = diff_attention(aq, ak, av, da_lambda[l], da_norm_w[l], l)
        merged = jax.nn.sigmoid(ga) * (o_a @ w_branch_a[l]) + jax.nn.sigmoid(gb) * (o_b @ w_branch_b[l])
        x = layer_norm(DEEPNORM_ALPHA * x + merged @ w_out[l], ln_g[l, 0], ln_b[l, 0])
        ffn = (jax.nn.silu(x @ w_gate[l]) * (x @ w_up[l])) @ w_down[l]
        x = layer_norm(DEEPNORM_ALPHA * x + ffn, ln_g[l, 1], ln_b[l, 1])
    return x


_drawn_inputs = setup_inputs


def setup_inputs(seed=0):
    import zlib

    import numpy as np

    out = dict(_drawn_inputs(seed))
    spreads = {}
    factors = {'a_log': 3.048, 'dn_norm_w': 8.0, 'da_lambda': 3.354, 'da_norm_w': 8.0}
    for name, (base, spread) in spreads.items():
        noise = np.random.default_rng([zlib.crc32(name.encode()), seed]).standard_normal(out[name].shape)
        drawn = base * np.exp(spread * noise) if base else spread * noise
        out[name] = __import__('jax').numpy.asarray(drawn.astype(out[name].dtype))
    for name, factor in factors.items():
        out[name] = (out[name] * factor).astype(out[name].dtype)
    return out
```

```python
import math
from contextlib import ExitStack

import numpy as np

import concourse.bass as bass
from concourse import mybir

F32 = mybir.dt.float32
I32 = mybir.dt.int32
F32R = mybir.dt.float32r
ALU = mybir.AluOpType
ACT = mybir.ActivationFunctionType
X = mybir.AxisListType.X

P = 128
D = 2048
SEQ = 256
TOK = SEQ // P
KC = D // P
HEADS = 16
HB = 4
NB = HEADS // HB
CH = 64
CONV = 4
D_FF = -(-8 * D // (3 * 256)) * 256
NG = 512
TK = 2
CONV_SLOTS = [(10, 12), (18, 20), (28, 30)]
DA_TURN = [(19, 21), (25, 27)]
DA_TURN_FIRST = [(10, 12), (18, 20)]
CONV_LINKS, DN_LINKS, DA_LINKS = 43, 67, 69
TPG = KC // TK
RING = 4
AHEAD = 3
ALPHA = 2.0 ** 0.25
LAMBDA_INIT = 0.8 - 0.6 * math.exp(0.0)
LN_EPS = 1e-5
RMS_EPS = 1e-6
FG = D_FF // NG
PIECES = [(0, 4), (4, 8), (8, FG)]
BODY = 4 * TPG

N_DN, N_DA = 0, NB * BODY
N_GB = N_DA + NB * BODY
N_BR = N_GB + BODY
N_OUT = N_BR + 2 * BODY
N_FFN = N_OUT + BODY
N_TILES = N_FFN + 2 * TPG * FG + 4 * (D_FF // P // TK)
LEVELS = 6

CONST = {}
_at = 0
for _n, _w in [("ident", P), ("after", P), ("same", P), ("upto", CH), ("eye", CH), ("incl", CH),
               ("level", LEVELS * CH), ("negdist", 3 * P), ("slopes", HEADS)]:
    CONST[_n] = (_at, _at + _w)
    _at += _w
NCONST = _at
PARAM = {}
_at = 0
for _n, _w in [("conv", NB * 3 * HB * CONV), ("dnw", P), ("daw", P), ("dt", HEADS), ("alog", HEADS)]:
    PARAM[_n] = (_at, _at + _w)
    _at += _w
NPARAM = _at
SC = {"beta": (0, 8), "g": (8, 16), "eg": (16, 24), "tail": (24, 32), "total": (32, 48)}
NSC = 48


def build(nc, xT, xrow, weights, w_ab, consts, early, params, lam_in, ln_in, out):
    ctx = ExitStack()

    def sb(name, shape, dt=F32):
        return ctx.enter_context(nc.sbuf_tensor(name, shape, dt))

    def sem(name):
        return ctx.enter_context(nc.semaphore(name))

    with ctx:
        act_x = sb("act_x", [P, 2, KC, SEQ], F32R)
        act_a = sb("act_a", [P, 2, KC, SEQ], F32R)
        dn = ExitStack()

        def tmp(name, shape):
            return dn.enter_context(nc.sbuf_tensor(name, shape, F32))

        cT = tmp("cT", [P, 3, HB, SEQ])
        kn = tmp("kn", [P, 2, HB, P])
        ktail = tmp("ktail", [P, 2, HB, P])
        vtok = tmp("vtok", [P, 2, HB, P])
        knT_o = tmp("knT_o", [P, 2, HB, P])
        u_sq = tmp("u_sq", [P, 2, HB, P])
        w_sq = tmp("w_sq", [P, 2 * HB * P])
        decm = tmp("decm", [P, 8, CH])
        AT = tmp("AT", [P, 8, CH])
        QKT = tmp("QKT", [P, 8, CH])
        T = tmp("T", [P, 8, CH])
        TT = tmp("TT", [P, 8, CH])
        Pm = tmp("Pm", [P, 8, CH])
        TTb = tmp("TTb", [P, 8, CH])
        TTg = tmp("TTg", [P, 8, CH])
        S = tmp("S", [P, HB, P])
        vn = tmp("vn", [P, HB, P])
        zs = tmp("zs", [P, 2, NG])
        dn.close()
        act_b = sb("act_b", [P, 2, KC, SEQ], F32R)
        gates = sb("gates", [P, 2, TOK, D])
        y = gates[:, 0]
        lnp = gates[:, 1]

        raw = sb("raw", [P, RING, TK, NG])
        whi = sb("whi", [P, RING, TK, NG], F32R)
        wlo = sb("wlo", [P, RING, TK, NG], F32R)
        cst = sb("cst", [P, NCONST])
        par = sb("par", [P, NPARAM])
        scal = sb("scal", [P, NB, NSC])
        cur = sb("cur", [P, NSC])
        cw = sb("cw", [P, 3, HB, CONV])
        sm = sb("sm", [P, 72])
        lam = sb("lam", [P, 2])
        g_all = sb("g_all", [P, TOK * HEADS])
        pz = sb("pz", [P, 4, TOK * HEADS])
        lnst = sb("lnst", [P, TOK, 4, 6])
        lnmv = sb("lnmv", [P, TOK, 2])
        hraw = sb("hraw", [P, TOK, NG])
        qT = sb("qT", [P, HB, SEQ])
        kT = sb("kT", [P, HB, SEQ])
        vda = sb("vda", [P, TOK, NG])
        pr = sb("pr", [P, 2, 3 * P])
        pT = sb("pT", [P, 3 * P])
        oh = sb("oh", [P, TOK, P])

        pg = [[ctx.enter_context(nc.psum_tensor(f"pg{a}{t}", [P, NG], F32)) for t in range(TOK)] for a in range(2)]
        B = [ctx.enter_context(nc.psum_tensor(f"B{i}", [P, NG], F32)) for i in range(4)]

        def c(name):
            a, b = CONST[name]
            return cst[:, a:b]

        def s_(name):
            a, b = SC[name]
            return cur[:, a:b]

        ident = c("ident")
        ones = c("same")
        B4 = [b[:, :].rearrange("p (h d) -> p h d", h=HB) for b in B]
        B8 = [b[:, :].rearrange("p (h d) -> p h d", h=8) for b in B]

        def bc(ap, n):
            return ap.unsqueeze(2).broadcast_to([P, ap.shape[1], n])

        def rep(ap, m):
            return ap.unsqueeze(1).broadcast_to([P, m, ap.shape[1]])

        xt4 = [cT[:, 0], cT[:, 1], cT[:, 2],
               kn[:, :, :, :].rearrange("p t h d -> p (t h d)").rearrange("p (h s) -> p h s", h=HB)]
        xres = [b[:, :, :].rearrange("p h s -> p (h s)").rearrange("p (t n) -> p t n", t=TOK) for b in (qT, kT)]
        upto_r, sel0, sel1 = (u_sq[:, 0, i, :] for i in range(3))
        kn8, ktail8, u8, zs8 = (b.rearrange("p (i d) -> p i d", d=P) for b in (
            kn[:, :, :, :].rearrange("p t h d -> p (t h d)"), ktail[:, :, :, :].rearrange("p t h d -> p (t h d)"),
            u_sq[:, :, :, :].rearrange("p t h d -> p (t h d)"), zs[:, :, :].rearrange("p t n -> p (t n)")))

        raw_full = [sem(f"raw_full{i}") for i in range(RING)]
        hi_done = sem("hi_done")
        lo_done = sem("lo_done")
        tile_used = sem("tile_used")
        evac = [sem("evac_even"), sem("evac_odd")]
        xt_full = [sem(f"xt_full{i}") for i in range(4)]
        const_full = sem("const_full")
        ln_full = sem("ln_full")
        xres_full = [sem("xres_full0"), sem("xres_full1")]
        xres_used = sem("xres_used")
        out_full = sem("out_full")
        x_hi = sem("x_hi")
        x_lo = sem("x_lo")
        once = """pe_passed pe_ab pe_sc0 act_pro dve_pro dve_sc0 act_tot dve_lam act_lam
            dve_x1 pe_x1T act_x1T dve_x1T act_var dve_xc dve_out pro_chain ln_chain""".split()
        counted = """pe_conv dve_conv act_silu
            pe_ktok pe_dt pe_qss pe_v pe_knT pe_kq pe_br pe_p pe_t pe_u pe_w pe_a pe_b pe_oT
            act_sqk act_sqq act_decay act_v act_knT act_br act_u act_w act_osq act_oT
            dve_rows dve_kn dve_rq dve_at dve_p dve_t dve_tb dve_s dve_vn dve_o1 dve_o2 dve_oh dve_oT
            pe_qkT act_qkT pe_s dve_s1 dve_mx act_exp dve_pd pe_pT act_pT pe_pv act_oss dve_oh2 pe_oT2
            act_oT2 dve_oT2 dve_m pe_mT act_mT dve_mT conv_chain dn_chain da_chain""".split()
        N = {n: sem(n) for n in once + counted}

        class Chain:

            def __init__(self, eng, sm_, base=0):
                self.eng, self.sem, self.base, self.n = eng, sm_, base, 0

            def __call__(self, ins):
                self.n += 1
                ins.then_inc(self.sem, 1)
                self.eng.wait_ge(self.sem, self.base + self.n)

        def hi(buf, k, n, t0=0, t1=SEQ):
            return buf[:, 0, bass.ds(k, n), t0:t1]

        def lo(buf, k, n, t0=0, t1=SEQ):
            return buf[:, 1, bass.ds(k, n), t0:t1]


        def ffn_walk(eng, up, down, turn):
            n, g, cnt = N_FFN, 4 * NB + 2 + NB + 2, NB
            up(n, g, cnt, None)
            with eng.Fori(1, 4) as f:
                up(n + 2 * TPG * f, g + f, cnt + f, (act_x, 4 * (f - 1)))
            up(n + 2 * TPG * 4, g + 4, cnt + 4, (act_x, 12))
            n, g, cnt = n + 2 * TPG * 5, g + 5, cnt + 5
            turn(cnt, (act_b, 0))
            down(0, n, g, TPG, act_x)
            n, g = n + 4 * TPG, g + 2
            up(n, g, cnt, None)
            with eng.Fori(1, 3) as f:
                up(n + 2 * TPG * f, g + f, cnt + f, (act_b, 4 * f))
            up(n + 2 * TPG * 3, g + 3, cnt + 3, (act_b, 12))
            n, g, cnt = n + 2 * TPG * 4, g + 4, cnt + 4
            turn(cnt, (act_x, 0))
            down(1, n, g, TPG, act_b)
            n, g = n + 4 * TPG, g + 2
            up(n, g, cnt, None)
            up(n + 2 * TPG, g + 1, cnt + 1, (act_x, 4))
            n, g, cnt = n + 4 * TPG, g + 2, cnt + 2
            turn(cnt, (act_x, 8))
            down(2, n, g, 2 * (FG - 8), act_x)

        block = ctx.enter_context(nc.Block())

        @block.sync
        def _(sp):
            for i in range(4):
                sp.dma_start(xt4[i], xT[i]).then_inc(xt_full[i], 16)
                if i == 0:
                    sp.dma_start(cst[:, :], consts).then_inc(const_full, 16)
                    sp.dma_start(par[:, :], params).then_inc(const_full, 16)
                    sp.dma_start(u_sq[:, 0, 0:3, :].rearrange("p a b -> p (a b)"), early).then_inc(const_full, 16)
                    sp.dma_start(w_sq[:, 0:NG], w_ab).then_inc(const_full, 16)
                    sp.dma_start(vda[:, 0, 0:4 * CH], lam_in).then_inc(const_full, 16)
            total = weights.shape[0]
            for n in range(RING):
                sp.dma_start(raw[:, n].rearrange("p k n -> p (k n)"), weights[n]).then_inc(raw_full[n], 16)
            for n in counted:
                sp.sem_inc(N[n], 1)

            def later(m):
                for r in range(RING):
                    sp.wait_ge(hi_done, RING * m + r - RING + 1)
                    sp.wait_ge(lo_done, RING * m + r - RING + 1)
                    sp.dma_start(raw[:, r].rearrange("p k n -> p (k n)"),
                                 weights[bass.ds(RING * m + r, 1)].rearrange("o p n -> (o p) n")
                                 ).then_inc(raw_full[r], 16)
            out_m = N_OUT // RING
            with sp.Fori(1, out_m) as m:
                later(m)
            sp.wait_ge(N["dve_oT2"], 1 + HEADS)
            for g in range(2):
                sp.dma_start(xres[g], xrow[g]).then_inc(xres_full[g], 16)
            at = out_m
            for g in range(2, 4):
                with sp.Fori(at, out_m + 2 * g - 1) as m:
                    later(m)
                at = out_m + 2 * g - 1
                sp.wait_ge(xres_used, g - 1)
                sp.dma_start(xres[g % 2], xrow[g]).then_inc(xres_full[g % 2], 16)
            sp.wait_ge(N["dve_m"], 1 + NB)
            sp.dma_start(lnp, ln_in[0]).then_inc(ln_full, 16)
            with sp.Fori(at, total // RING) as m:
                later(m)
            sp.wait_ge(N["dve_x1"], 1)
            sp.dma_start(lnp, ln_in[1]).then_inc(ln_full, 16)
            for t in range(TOK):
                sp.wait_ge(N["dve_out"], t + 1)
                sp.dma_start(out[0, t * P:(t + 1) * P, :], y[:, t, :]).then_inc(out_full, 16)
            sp.wait_ge(out_full, 16 * TOK)


        @block.tensor
        def _(pe):
            def mm(o, l, r, start=True, stop=True):
                return nc.tensor.matmul(o, l, r, start=start, stop=stop)

            def gemm_tile(n, q, a, k0, pair, last):
                r = q % RING
                pe.wait_ge(hi_done, n + 1)
                pe.wait_ge(lo_done, n + 1)
                for k in range(TK):
                    for t in range(TOK):
                        xh = a[:, 0, k0 + k, t * P:(t + 1) * P]
                        xl = a[:, 1, k0 + k, t * P:(t + 1) * P]
                        first = k0 + k == 0
                        mm(pg[pair][t][:, :], xh, whi[:, r, k, :], first, False)
                        mm(pg[pair][t][:, :], xh, wlo[:, r, k, :], False, False)
                        end = mm(pg[pair][t][:, :], xl, whi[:, r, k, :], False, last and k == TK - 1)
                end.then_inc(tile_used, 1)

            pe.wait_ge(const_full, 80)
            for t in range(TOK):
                for k in range(KC):
                    if t == 0 and k % 4 == 0:
                        pe.wait_ge(xt_full[k // 4], 16)
                    last = mm(B[t][:, 0:32], xt4[k // 4][:, k % 4, t * P:(t + 1) * P],
                              w_sq[:, 32 * k:32 * k + 32], k == 0, k == KC - 1)
            last.then_inc(N["pe_ab"], 1)
            pe.wait_ge(N["dve_pro"], 1)
            mm(B[2][:, 0:32], upto_r, g_all[:, :])
            mm(B[2][:, 32:64], c("after"), g_all[:, :])
            mm(B[2][:, 64:96], sel0, g_all[:, :])
            mm(B[2][:, 96:128], sel1, g_all[:, :]).then_inc(N["pe_sc0"], 1)

            def turn_conv(j, kind, half):
                pe.wait_ge(evac[[0, 1, 0][kind]], 2 * j + [1, 1, 2][kind])
                pe.wait_ge(N["dve_conv"], 1 + 6 * j + 2 * kind + half)
                for i in range(2):
                    for t in range(TOK):
                        h = 2 * half + i
                        last = nc.tensor.transpose(B[0][:, i * SEQ + t * P:i * SEQ + (t + 1) * P],
                                                   hraw[:, t, h * P:(h + 1) * P], ident)
                last.then_inc(N["pe_conv"], 1)

            def dn_conv(j, s):
                for kind, slots in enumerate(CONV_SLOTS):
                    if s in slots:
                        turn_conv(j, kind, slots.index(s))

            def waits_end():
                pe.sem_inc(N["pe_passed"], 1)

            def dn_mix(j, s):
                if s == 0:
                    pe.wait_ge(N["act_silu"], 1 + 3 * j + 1)
                    pe.wait_ge(N["dve_oT"], 1 + 2 * j)
                    for t in range(TOK):
                        for h in range(HB):
                            last = nc.tensor.transpose(B4[1 + t][:, h, :], cT[:, 0, h, t * P:(t + 1) * P], ident)
                    last.then_inc(N["pe_ktok"], 1)
                if s == 1:
                    pe.wait_ge(N["dve_rows"], 1 + j + 1)
                    mm(B[3][:, :], c("after"), Pm[:, :, :].rearrange("p a b -> p (a b)")).then_inc(N["pe_dt"], 1)
                if s == 2:
                    pe.wait_ge(N["act_decay"], 1 + j + 1)
                    pe.wait_ge(N["act_sqq"], 1 + j + 1)
                    for t in range(TOK):
                        for h in range(HB):
                            last = mm(B[3][:, 4 * t + h:4 * t + h + 1],
                                      w_sq[:, h * SEQ + t * P:h * SEQ + (t + 1) * P], c("incl")[:, CH - 1:CH])
                    last.then_inc(N["pe_qss"], 1)
                if s in (3, 4):
                    t = s - 3
                    if t == 0:
                        pe.wait_ge(N["act_silu"], 1 + 3 * j + 2)
                        pe.wait_ge(N["dve_rq"], 1 + j + 1)
                    else:
                        pe.wait_ge(N["act_v"], 1 + 2 * j + 1)
                    for h in range(HB):
                        last = nc.tensor.transpose(B4[3][:, h, :], cT[:, 1, h, t * P:(t + 1) * P], ident)
                    last.then_inc(N["pe_v"], 1)
                if s == 3:
                    pe.wait_ge(N["dve_kn"], 1 + j + 1)
                    for t in range(TOK):
                        for h in range(HB):
                            last = nc.tensor.transpose(B4[1 + t][:, h, :], kn[:, t, h, :], ident)
                    last.then_inc(N["pe_knT"], 1)
                if s == 5:
                    pe.wait_ge(N["act_knT"], 1 + j + 1)
                    for t in range(TOK):
                        for h in range(HB):
                            for p in range(2):
                                kc = knT_o[:, t, h, p * CH:(p + 1) * CH]
                                qc = cT[:, 2, h, t * P + p * CH:t * P + (p + 1) * CH]
                                mm(B8[1][p * CH:(p + 1) * CH, 4 * t + h, :], kc, kc)
                                last = mm(B8[2][p * CH:(p + 1) * CH, 4 * t + h, :], kc, qc)
                    last.then_inc(N["pe_kq"], 1)
                if s == 6:
                    pe.wait_ge(N["act_v"], 1 + 2 * j + 2)
                    mm(B[3][:, :], c("same"), TTb[:, :, :].rearrange("p a b -> p (a b)")).then_inc(N["pe_br"], 1)
                if 7 <= s < 7 + 2 * LEVELS:
                    lv, odd = divmod(s - 7, 2)
                    if not odd:
                        if lv == 0:
                            pe.wait_ge(N["dve_at"], 1 + j + 1)
                        pe.wait_ge(N["dve_t"], 1 + LEVELS * j + lv)
                        waits_end()
                        for i in range(8):
                            for p in range(2):
                                a = slice(p * CH, (p + 1) * CH)
                                last = mm(B8[1][a, i, :], AT[a, i, :], T[a, i, :])
                        last.then_inc(N["pe_p"], 1)
                    else:
                        pe.wait_ge(N["dve_p"], 1 + LEVELS * j + lv + 1)
                        waits_end()
                        for i in range(8):
                            for p in range(2):
                                a = slice(p * CH, (p + 1) * CH)
                                last = mm(B8[2][a, i, :], Pm[a, i, :], TT[a, i, :])
                                if lv < LEVELS - 1:
                                    last = mm(B8[3][a, i, :], TT[a, i, :], Pm[a, i, :])
                        last.then_inc(N["pe_t"], 1)
                if s == 19:
                    pe.wait_ge(N["dve_tb"], 1 + j + 1)
                    waits_end()
                    for t in range(TOK):
                        for h in range(HB):
                            for p in range(2):
                                a = slice(p * CH, (p + 1) * CH)
                                last = mm(B4[1 + t][a, h, :], TTb[a, 4 * t + h, :], vtok[a, t, h, :])
                    last.then_inc(N["pe_u"], 1)
                if s in (19, 20):
                    p = s - 19
                    if p:
                        pe.wait_ge(N["act_w"], 1 + 2 * j + 1)
                    a = slice(p * CH, (p + 1) * CH)
                    for t in range(TOK):
                        for h in range(HB):
                            last = mm(B8[3][:, 4 * t + h, :], kn[a, t, h, :], TTg[a, 4 * t + h, :])
                    last.then_inc(N["pe_w"], 1)
                if 21 <= s < 29:
                    ck, odd = divmod(s - 21, 2)
                    t, p = divmod(ck, 2)
                    a = slice(p * CH, (p + 1) * CH)
                    if not odd:
                        if ck == 0:
                            pe.wait_ge(N["act_u"], 1 + j + 1)
                            pe.wait_ge(N["act_w"], 1 + 2 * j + 2)
                        if ck == 2:
                            pe.wait_ge(N["dve_o1"], 1 + 2 * j + 1)
                        pe.wait_ge(N["dve_s"], 1 + 4 * j + ck + 1)
                        for h in range(HB):
                            wv = w_sq[:, (p * 8 + 4 * t + h) * CH:(p * 8 + 4 * t + h + 1) * CH]
                            mm(B4[1][a, h, :], wv, S[:, h, :])
                            last = mm(B4[2][a, h, :], cT[:, 2, h, ck * CH:(ck + 1) * CH], S[:, h, :])
                        last.then_inc(N["pe_a"], 1)
                    else:
                        if ck == 2:
                            pe.wait_ge(N["dve_o2"], 1 + 2 * j + 1)
                        pe.wait_ge(N["dve_vn"], 1 + 4 * j + ck + 1)
                        waits_end()
                        for h in range(HB):
                            last = mm(B4[3][a, h, :], QKT[a, 4 * t + h, :], vn[a, h, :])
                            if ck < 3:
                                last = mm(B4[1][:, h, :], ktail[a, t, h, :], vn[a, h, :])
                        last.then_inc(N["pe_b"], 1)
                if s in (29, 31):
                    t = (s - 29) // 2
                    pe.wait_ge(N["dve_oh"], 1 + 2 * j + t + 1)
                    for h in range(HB):
                        last = nc.tensor.transpose(B4[1 + t][:, h, :], knT_o[:, t, h, :], ident)
                    last.then_inc(N["pe_oT"], 1)

            def da_turn(j, which, half, e):
                pe.wait_ge(evac[e[0]], e[1])
                pe.wait_ge(N["act_qkT"], 1 + 4 * j + 2 * which + half)
                pe.wait_ge(N["dve_oT2"], 1 + HB * j)
                for i in range(2):
                    for t in range(TOK):
                        h = 2 * half + i
                        last = nc.tensor.transpose(B[0][:, i * SEQ + t * P:i * SEQ + (t + 1) * P],
                                                   hraw[:, t, h * P:(h + 1) * P], ident)
                last.then_inc(N["pe_qkT"], 1)

            def da_mix(j, s):
                h, step = divmod(s, 4)
                if h < HB and step == 0:
                    pe.wait_ge(N["act_qkT"], 1 + 4 * j + 4)
                    pe.wait_ge(N["dve_s1"], 1 + HB * j + h)
                    for t in range(TOK):
                        for m in range(2):
                            a = slice(m * CH, (m + 1) * CH)
                            last = mm(B[1 + m][:, t * P:t * P + (t + 1) * P],
                                      qT[a, h, t * P:(t + 1) * P], kT[a, h, 0:(t + 1) * P])
                    last.then_inc(N["pe_s"], 1)
                if h < HB and step == 2:
                    pe.wait_ge(N["dve_pd"], 1 + HB * j + h + 1)
                    pe.wait_ge(N["dve_oh2"], 1 + HB * j + h)
                    for i in range(3):
                        last = nc.tensor.transpose(B[3][:, i * P:(i + 1) * P], pr[:, 0, i * P:(i + 1) * P], ident)
                    last.then_inc(N["pe_pT"], 1)
                if h < HB and step == 3:
                    pe.wait_ge(N["act_pT"], 1 + HB * j + h + 1)
                    mm(B[3][:, 0:P], pT[:, 0:P], vda[:, 0, h * P:(h + 1) * P])
                    mm(B[3][:, P:2 * P], pT[:, P:2 * P], vda[:, 0, h * P:(h + 1) * P], True, False)
                    mm(B[3][:, P:2 * P], pT[:, 2 * P:3 * P], vda[:, 1, h * P:(h + 1) * P], False, True
                       ).then_inc(N["pe_pv"], 1)
                h, step = divmod(s - 5, 4)
                if 0 <= h < HB and step == 0:
                    pe.wait_ge(N["dve_oh2"], 1 + HB * j + h + 1)
                    pe.wait_ge(N["dve_oT2"], 1 + HB * j + h)
                    for t in range(TOK):
                        last = nc.tensor.transpose(B[0][:, t * P:(t + 1) * P], oh[:, t, :], ident)
                    last.then_inc(N["pe_oT2"], 1)

            def turn_rows(cnt):
                pe.wait_ge(N["dve_m"], 1 + cnt + 1)
                pe.wait_ge(N["dve_mT"], 1 + cnt)
                for t in range(TOK):
                    for i in range(4):
                        last = nc.tensor.transpose(B4[t][:, i, :], hraw[:, t, i * P:(i + 1) * P], ident)
                last.then_inc(N["pe_mT"], 1)

            def body(n, g, a, mixes=(), regions=None):
                for i in range(4):
                    pair = i % 2
                    pe.wait_ge(evac[pair], g + i // 2)
                    for q in range(TPG):
                        s = i * TPG + q
                        gemm_tile(n + s, s, a, TK * q, pair, q == TPG - 1)
                        for mix in mixes:
                            mix(s)

            pe.wait_ge(x_hi, 4)
            pe.wait_ge(x_lo, 4)
            pe.wait_ge(N["act_tot"], 1)
            body(0, 0, act_x, [lambda s: dn_conv(0, s)])
            with pe.Fori(1, NB) as j:
                body(j * BODY, 2 * j, act_x, [lambda s: dn_mix(j - 1, s), lambda s: dn_conv(j, s)])

            def da_turns(j, s, first):
                for which, slots in enumerate(DA_TURN_FIRST if first else DA_TURN):
                    if s in slots:
                        g = which if first else which + 1
                        da_turn(j, which, slots.index(s), (g % 2, 2 * NB + 2 * j + g // 2 + 1))

            body(N_DA, 2 * NB, act_x, [lambda s: dn_mix(NB - 1, s), lambda s: da_turns(0, s, True)])
            pe.wait_ge(N["dve_oT"], 1 + 2 * NB)
            with pe.Fori(1, NB) as j:
                body(N_DA + j * BODY, 2 * NB + 2 * j, act_x,
                     [lambda s: da_mix(j - 1, s), lambda s: da_turns(j, s, False)])
            body(N_GB, 4 * NB, act_x, [lambda s: da_mix(NB - 1, s)])

            def pair_of_groups(n, g, regs, after):
                for i in range(2):
                    pe.wait_ge(evac[i], g)
                    for q in range(TPG):
                        gemm_tile(n + i * TPG + q, q, regs[i], TK * q, i, q == TPG - 1)
                        if i == 0 and q == 1 and after:
                            after()

            pe.wait_ge(N["dve_oT2"], 1 + HEADS)
            g0 = 4 * NB + 2
            pair_of_groups(N_BR, g0, (act_a, act_b), None)
            with pe.Fori(1, NB) as j:
                pair_of_groups(N_BR + 2 * TPG * j, g0 + j, (act_a, act_b), lambda: turn_rows(j - 1))
            turn_rows(NB - 1)
            pe.wait_ge(N["dve_mT"], 1 + NB)
            body(N_OUT, g0 + NB, act_x)

            def turn_x1(i):
                t, cq = divmod(i, 4)
                pe.wait_ge(N["dve_x1"], 1)
                if i >= 4:
                    pe.wait_ge(N["dve_x1T"], i - 3)
                for q in range(4):
                    last = nc.tensor.transpose(B4[i % 4][:, q, :], y[:, t, (4 * cq + q) * P:(4 * cq + q + 1) * P],
                                               ident)
                last.then_inc(N["pe_x1T"], 1)
            for i in range(8):
                turn_x1(i)
            pe.wait_ge(N["dve_x1T"], 8)

            def up(n, g, cnt, place):
                pair_of_groups(n, g, (act_a, act_a), (lambda: turn_rows(cnt - 1)) if place else None)

            def down(piece, n, g, tiles, buf):
                with pe.Fori(0, 2) as i:
                    for e in range(2):
                        pe.wait_ge(evac[e], g + i)
                        for q in range(tiles):
                            gemm_tile(n + 2 * tiles * i + e * tiles + q, e * tiles + q, buf, TK * q, e,
                                      q == tiles - 1)

            def turn(cnt, place):
                turn_rows(cnt - 1)
                pe.wait_ge(N["dve_mT"], 1 + cnt)
            ffn_walk(pe, up, down, turn)


        @block.scalar
        def _(act):
            def copy(o, i, scale=1.0):
                return nc.scalar.activation(o, i, ACT.Copy, scale=scale)

            def split(n, s):
                if isinstance(n, int) and n + s + AHEAD >= N_TILES:
                    return
                rounds, r = divmod(s + AHEAD, RING)
                act.wait_ge(raw_full[r], (16 // RING) * n + 16 * (rounds + 1))
                act.wait_ge(tile_used, n + s)
                copy(whi[:, r], raw[:, r]).then_inc(hi_done, 1)

            for i in range(4):
                act.wait_ge(xt_full[i], 16)
                copy(act_x[:, 0, 4 * i:4 * i + 4, :], xt4[i]).then_inc(x_hi, 1)
            for s in range(-AHEAD, 0):
                act.wait_ge(raw_full[s + AHEAD], 16)
                copy(whi[:, s + AHEAD], raw[:, s + AHEAD]).then_inc(hi_done, 1)
            act.wait_ge(const_full, 80)
            act.wait_ge(N["pe_ab"], 1)
            for t in range(TOK):
                nc.scalar.activation(scal[:, :, 4 * t:4 * t + 4],
                                     B[t][:, 0:HEADS].rearrange("p (j h) -> p j h", h=HB), ACT.Sigmoid
                                     ).then_inc(N["act_lam"], 1)
            act.wait_ge(N["dve_sc0"], 1)
            nc.scalar.activation(pz[:, 1, :], pz[:, 1, :], ACT.Exp, scale=-1.0)
            nc.scalar.activation(pz[:, 3, 0:HEADS], par[:, slice(*PARAM["alog"])], ACT.Exp).then_inc(N["act_pro"], 1)
            act.wait_ge(N["dve_lam"], 1)
            nc.scalar.activation(lam[:, :], lam[:, :], ACT.Exp).then_inc(N["act_lam"], 1)
            act.wait_ge(N["pe_sc0"], 1)
            for t in range(TOK):
                for f, at in (("eg", 0), ("tail", 32)):
                    a0 = SC[f][0] + 4 * t
                    nc.scalar.activation(scal[:, :, a0:a0 + 4], B[2][:, at + HEADS * t:at + HEADS * t + HEADS]
                                         .rearrange("p (j h) -> p j h", h=HB), ACT.Exp)
                for p in range(2):
                    a0 = SC["total"][0] + 8 * t + 4 * p
                    at = 64 + 32 * p + HEADS * t
                    last = nc.scalar.activation(scal[:, :, a0:a0 + 4], B[2][:, at:at + HEADS].rearrange(
                        "p (j h) -> p j h", h=HB), ACT.Exp)
            last.then_inc(N["act_tot"], 1)

            def rows_out(pair, dst, func=ACT.Copy, dyn=None):
                for t in range(TOK):
                    last = nc.scalar.activation(dst(t), pg[pair][t][:, :], func)
                last.then_inc(evac[pair], 1)

            def dn_evac(n, i, j):
                act.wait_ge(tile_used, n)
                if i < 3:
                    act.wait_ge(N["pe_conv"], 1 + 6 * j + 2 * i)
                    rows_out(i % 2, lambda t: hraw[:, t, :])
                else:
                    act.wait_ge(N["dve_oh"], 1 + 2 * j)
                    rows_out(1, lambda t: zs[:, t, :], ACT.Silu)

            def dn_conv(j, s):
                for kind, slots in enumerate(CONV_SLOTS):
                    if s == slots[1]:
                        act.wait_ge(N["dve_conv"], 1 + 6 * j + 2 * kind + 2)
                        nc.scalar.activation(cT[:, kind], cT[:, kind], ACT.Silu).then_inc(N["act_silu"], 1)

            def dn_mix(j, s):
                if s == 0:
                    act.wait_ge(N["pe_a"], 1 + 4 * j)
                    act.wait_ge(N["act_silu"], 1 + 3 * j + 3)
                    nc.scalar.activation(w_sq[:, :], cT[:, 2].rearrange("p h s -> p (h s)"), ACT.Square
                                         ).then_inc(N["act_sqq"], 1)
                    act.wait_ge(N["pe_ktok"], 1 + j + 1)
                    act.wait_ge(N["dve_vn"], 1 + 4 * j)
                    for t in range(TOK):
                        last = nc.scalar.activation(u_sq[:, t], B4[1 + t], ACT.Square)
                    last.then_inc(N["act_sqk"], 1)
                if s == 1:
                    act.wait_ge(N["pe_dt"], 1 + j + 1)
                    act.wait_ge(N["dve_at"], 1 + j)
                    nc.scalar.activation(decm[:, :, :], B8[3], ACT.Exp).then_inc(N["act_decay"], 1)
                if s in (3, 4):
                    t = s - 3
                    act.wait_ge(N["pe_v"], 1 + 2 * j + t + 1)
                    act.wait_ge(N["pe_u"], 1 + j)
                    copy(vtok[:, t], B4[3]).then_inc(N["act_v"], 1)
                if s == 3:
                    act.wait_ge(N["pe_knT"], 1 + j + 1)
                    act.wait_ge(N["pe_oT"], 1 + 2 * j)
                    for t in range(TOK):
                        last = copy(knT_o[:, t], B4[1 + t])
                    last.then_inc(N["act_knT"], 1)
                if s == 6:
                    act.wait_ge(N["pe_br"], 1 + j + 1)
                    act.wait_ge(N["pe_w"], 1 + 2 * j)
                    copy(TTg[:, :, :], B8[3]).then_inc(N["act_br"], 1)
                if s == 19:
                    act.wait_ge(N["pe_u"], 1 + j + 1)
                    act.wait_ge(N["dve_kn"], 1 + j + 1)
                    for t in range(TOK):
                        last = copy(u_sq[:, t], B4[1 + t])
                    last.then_inc(N["act_u"], 1)
                if s in (19, 20):
                    p = s - 19
                    act.wait_ge(N["pe_w"], 1 + 2 * j + p + 1)
                    copy(w_sq[:, p * NG:(p + 1) * NG], B[3][:, :]).then_inc(N["act_w"], 1)
                if s in (25, 29):
                    t = (s - 25) // 4
                    act.wait_ge(N["dve_o2"], 1 + 2 * j + t + 1)
                    nc.scalar.activation(kn[:, t], knT_o[:, t], ACT.Square).then_inc(N["act_osq"], 1)
                if s in (29, 31):
                    t = (s - 29) // 2
                    act.wait_ge(N["pe_oT"], 1 + 2 * j + t + 1)
                    copy(hi(act_a, HB * j, HB, t * P, (t + 1) * P), B4[1 + t]).then_inc(N["act_oT"], 1)

            def body(n, evac_fn, mixes=()):
                for s in range(BODY):
                    split(n, s)
                    for mix in mixes:
                        mix(s)
                    if s % TPG == TPG - 1:
                        evac_fn(n + s + 1, s // TPG)

            body(0, lambda n, i: dn_evac(n, i, 0), [lambda s: dn_conv(0, s)])
            with act.Fori(1, NB) as j:
                body(BODY * j, lambda n, i: dn_evac(n, i, j), [lambda s: dn_mix(j - 1, s), lambda s: dn_conv(j, s)])

            def da_evac(n, i, j, first):
                act.wait_ge(tile_used, n)
                what = ("q", "k", "v", "g")[i] if first else ("g", "q", "k", "v")[i]
                if what == "q":
                    act.wait_ge(N["pe_conv"], 1 + 6 * NB)
                    act.wait_ge(N["pe_qkT"], 1 + 4 * j)
                    rows_out(i % 2, lambda t: hraw[:, t, :])
                if what == "k":
                    act.wait_ge(N["pe_qkT"], 1 + 4 * j + 2)
                    rows_out(i % 2, lambda t: hraw[:, t, :])
                if what == "v":
                    act.wait_ge(N["pe_pv"], 1 + HB * j)
                    rows_out(i % 2, lambda t: vda[:, t, :])
                if what == "g":
                    act.wait_ge(N["dve_oT"], 1 + 2 * NB)
                    rows_out(i % 2, lambda t: gates[:, 0, t, bass.ds(NG * j, NG)], ACT.Sigmoid)

            def da_turns(j, s, first):
                for which, slots in enumerate(DA_TURN_FIRST if first else DA_TURN):
                    if s in slots:
                        half = slots.index(s)
                        act.wait_ge(N["pe_qkT"], 1 + 4 * j + 2 * which + half + 1)
                        act.wait_ge(N["pe_s"], 1 + HB * j)
                        copy((qT, kT)[which][:, 2 * half:2 * half + 2, :],
                             B[0][:, :].rearrange("p (h s) -> p h s", h=2), CH ** -0.5 if which == 0 else 1.0
                             ).then_inc(N["act_qkT"], 1)

            def da_mix(j, s):
                h, step = divmod(s, 4)
                if h < HB and step == 0:
                    act.wait_ge(N["dve_mx"], 1 + HB * j + h + 1)
                    for r, (a, b) in enumerate([(0, P), (P, 3 * P)]):
                        for m in range(2):
                            i = 2 * r + m
                            last = nc.scalar.activation(pr[:, m, a:b], pr[:, m, a:b], ACT.Exp,
                                                        bias=sm[:, 28 + i:29 + i], accum_out=sm[:, 32 + i:33 + i])
                    last.then_inc(N["act_exp"], 1)
                if h < HB and step == 2:
                    act.wait_ge(N["pe_pT"], 1 + HB * j + h + 1)
                    act.wait_ge(N["pe_pv"], 1 + HB * j + h)
                    copy(pT[:, :], B[3][:, 0:3 * P]).then_inc(N["act_pT"], 1)
                if h < HB and step == 3:
                    act.wait_ge(N["pe_pv"], 1 + HB * j + h + 1)
                    for t in range(TOK):
                        last = nc.scalar.activation(pr[:, 1, t * P:(t + 1) * P], B[3][:, t * P:(t + 1) * P],
                                                    ACT.Square, accum_out=sm[:, 40 + t:41 + t])
                    last.then_inc(N["act_oss"], 1)
                h, step = divmod(s - 5, 4)
                if 0 <= h < HB and step == 0:
                    act.wait_ge(N["pe_oT2"], 1 + HB * j + h + 1)
                    copy(hi(act_b, HB * j + h, 1), B[0][:, 0:SEQ].unsqueeze(1)).then_inc(N["act_oT2"], 1)

            body(N_DA, lambda n, i: da_evac(n, i, 0, True),
                 [lambda s: dn_mix(NB - 1, s), lambda s: da_turns(0, s, True)])
            with act.Fori(1, NB) as j:
                body(N_DA + BODY * j, lambda n, i: da_evac(n, i, j, False),
                     [lambda s: da_mix(j - 1, s), lambda s: da_turns(j, s, False)])

            def gb_evac(n, i):
                act.wait_ge(tile_used, n)
                rows_out(i % 2, lambda t: gates[:, 1, t, NG * i:NG * i + NG], ACT.Sigmoid)
            body(N_GB, gb_evac, [lambda s: da_mix(NB - 1, s)])

            def turn_rows(cnt, place):
                buf, k = place
                act.wait_ge(N["pe_mT"], 1 + cnt + 1)
                for t in range(TOK):
                    copy(hi(buf, k, 4, t * P, (t + 1) * P), B4[t]).then_inc(N["act_mT"], 1)

            def pair_of_groups(n, after):
                for s in range(2 * TPG):
                    split(n, s)
                    if s == 1 and after:
                        after()

            pair_of_groups(N_BR, None)
            with act.Fori(1, NB) as j:
                pair_of_groups(N_BR + 2 * TPG * j, lambda: turn_rows(j - 1, (act_x, 4 * (j - 1))))
            turn_rows(NB - 1, (act_x, 4 * (NB - 1)))
            for s in range(BODY):
                split(N_OUT, s)

            def split_x1():
                for i in range(8):
                    t, cq = divmod(i, 4)
                    act.wait_ge(N["pe_x1T"], i + 1)
                    copy(act_a[:, 0, 4 * cq:4 * cq + 4, t * P:(t + 1) * P], B4[i % 4]).then_inc(N["act_x1T"], 1)

            def normalize(ln):
                for t in range(TOK):
                    act.wait_ge(N["act_var"], 2 * ln + t + 1)
                    nc.scalar.activation(y[:, t, :], y[:, t, :], ACT.Identity, bias=lnmv[:, t, 0:1],
                                         scale=lnmv[:, t, 1:2]).then_inc(N["dve_xc"], 1)
            normalize(0)
            split_x1()

            def up(n, g, cnt, place):
                for s in range(2 * TPG):
                    split(n, s)
                    if s == 1 and place:
                        turn_rows(cnt - 1, place)
                    if s == TPG - 1:
                        act.wait_ge(tile_used, n + TPG)
                        act.wait_ge(N["dve_m"], 1 + cnt)
                        for t in range(TOK):
                            last = nc.scalar.activation(vda[:, t, :], pg[0][t][:, :], ACT.Silu)
                        last.then_inc(evac[0], 1)

            def down(piece, n, g, tiles, buf):
                if piece < 2:
                    with act.Fori(0, 2) as i:
                        for s in range(2 * tiles):
                            split(n + 2 * tiles * i, s)
                else:
                    for i in range(2):
                        for s in range(2 * tiles):
                            split(n + 2 * tiles * i, s)

            ffn_walk(act, up, down, lambda cnt, place: turn_rows(cnt - 1, place))
            normalize(1)

        @block.vector
        def _(dve):
            V = nc.vector

            def tt(o, a, b, op):
                return V.tensor_tensor(o, a, b, op)

            def ts(o, a, s1, op0, s2=None, op1=None):
                if op1 is None:
                    return V.tensor_scalar(o, a, s1, None, op0)
                return V.tensor_scalar(o, a, s1, s2, op0, op1)

            def stt(o, a, s, b, op0, op1):
                return V.scalar_tensor_tensor(out=o, in0=a, scalar=s, in1=b, op0=op0, op1=op1)

            def rsqrt(ch, o, x):
                a = sm[:, 64:64 + x.shape[1]]
                ch(V.tensor_single_scalar(o.bitcast(I32), x.bitcast(I32), 1, ALU.logical_shift_right))
                ch(ts(o.bitcast(I32), o.bitcast(I32), -1.0, ALU.mult, float(0x5F3759DF), ALU.add))
                for _ in range(3):
                    ch(stt(a, o, -0.5, o, ALU.mult, ALU.mult))
                    ch(tt(a, a, x, ALU.mult))
                    ch(stt(o, a, 1.5, o, ALU.add, ALU.mult))

            def split(n, s):
                if isinstance(n, int) and n + s + AHEAD >= N_TILES:
                    return
                r = (s + AHEAD) % RING
                dve.wait_ge(hi_done, n + s + AHEAD + 1)
                dve.wait_ge(tile_used, n + s)
                tt(wlo[:, r], raw[:, r], whi[:, r], ALU.subtract).then_inc(lo_done, 1)

            pro = Chain(dve, N["pro_chain"])
            for i in range(4):
                dve.wait_ge(x_hi, i + 1)
                tt(act_x[:, 1, 4 * i:4 * i + 4, :], xt4[i], act_x[:, 0, 4 * i:4 * i + 4, :], ALU.subtract
                   ).then_inc(x_lo, 1)
            for s in range(-AHEAD, 0):
                dve.wait_ge(hi_done, s + AHEAD + 1)
                tt(wlo[:, s + AHEAD], raw[:, s + AHEAD], whi[:, s + AHEAD], ALU.subtract).then_inc(lo_done, 1)
            dve.wait_ge(const_full, 80)
            lv = vda[:, 0, 0:4 * CH].rearrange("p (a b d) -> p a b d", a=2, b=2)
            pro(tt(vda[:, 1, 0:2 * CH].rearrange("p (a d) -> p a d", a=2), lv[:, :, 0, :], lv[:, :, 1, :], ALU.mult))
            V.tensor_reduce(lam[:, :], vda[:, 1, 0:2 * CH].rearrange("p (a d) -> p a d", a=2), X, ALU.add
                            ).then_inc(N["dve_lam"], 1)
            dve.wait_ge(N["pe_ab"], 1)
            dve.wait_ge(N["act_lam"], 2)
            for t in range(TOK):
                pro(tt(pz[:, 0, t * HEADS:(t + 1) * HEADS], B[t][:, HEADS:2 * HEADS], par[:, slice(*PARAM["dt"])],
                       ALU.add))
            stt(pz[:, 1, :], pz[:, 0, :], -1.0, pz[:, 0, :], ALU.mult, ALU.max).then_inc(N["dve_sc0"], 1)
            dve.wait_ge(N["act_pro"], 1)
            e, r, r2 = pz[:, 1, :], pz[:, 2, :], g_all[:, :]
            pro(ts(r, e, 2.0, ALU.add))
            pro(V.reciprocal(r, r))
            pro(tt(r, r, e, ALU.mult))
            pro(tt(r2, r, r, ALU.mult))
            pro(ts(e, r2, 2.0 / 17, ALU.mult, 2.0 / 15, ALU.add))
            for k in range(6, -1, -1):
                pro(tt(e, e, r2, ALU.mult))
                pro(ts(e, e, 2.0 / (2 * k + 1), ALU.add))
            pro(tt(e, e, r, ALU.mult))
            pro(stt(e, pz[:, 0, :], 0.0, e, ALU.max, ALU.add))
            for t in range(TOK):
                a = slice(t * HEADS, (t + 1) * HEADS)
                pro(stt(g_all[:, a], e[:, a], -1.0, pz[:, 3, 0:HEADS], ALU.mult, ALU.mult))
                g0 = SC["g"][0] + 4 * t
                pro(V.tensor_copy(scal[:, :, g0:g0 + 4], g_all[:, a].rearrange("p (j h) -> p j h", h=HB)))
            dve.wait_ge(N["act_lam"], 3)
            ts(lam[:, 0:1], lam[:, 0:1], lam[:, 1:2], ALU.subtract, LAMBDA_INIT, ALU.add).then_inc(N["dve_pro"], 1)
            dve.wait_ge(N["act_tot"], 1)

            def dn_conv(j, s):
                base = CONV_LINKS * j
                for kind, slots in enumerate(CONV_SLOTS):
                    if s not in slots:
                        continue
                    half = slots.index(s)
                    link = Chain(dve, N["conv_chain"], 1 + base + (7 * (2 * kind + half) + 1 if kind or half else 0))
                    if kind == 0 and half == 0:
                        a0 = PARAM["conv"][0]
                        link(V.tensor_copy(cw[:, :, :, :].rearrange("p k h c -> p (k h c)").unsqueeze(1),
                                           par[:, a0:a0 + NB * 48].rearrange("p (j c) -> p j c", j=NB)
                                           [:, bass.ds(j, 1), :]))
                    dve.wait_ge(N["pe_conv"], 1 + 6 * j + 2 * kind + half + 1)
                    if half == 0:
                        dve.wait_ge(N[("pe_ktok", "pe_v", "pe_a")[kind]], 1 + (1, 2, 4)[kind] * j)
                    for back in range(CONV):
                        for i in range(2):
                            h = 2 * half + i
                            w = cw[:, kind, h, CONV - 1 - back:CONV - back]
                            src = B[0][:, i * SEQ:(i + 1) * SEQ - back]
                            dst = cT[:, kind, h, back:SEQ]
                            if back == 0:
                                ins = ts(dst, src, w, ALU.mult)
                            else:
                                ins = stt(dst, src, w, dst, ALU.mult, ALU.add)
                            if back == CONV - 1 and i == 1:
                                ins.then_inc(N["dve_conv"], 1)
                            else:
                                link(ins)

            def dn_mix(j, s, ch):
                if s == 0:
                    dve.wait_ge(N["pe_t"], 1 + LEVELS * j)
                    dve.wait_ge(N["pe_u"], 1 + j)
                    ch(V.tensor_copy(cur[:, :].unsqueeze(1), scal[:, bass.ds(j, 1), :]))
                    tt(Pm[:, :, :], rep(c("upto"), 8), bc(s_("g"), CH), ALU.mult)
                    tt(TTb[:, :, :], rep(c("eye"), 8), bc(s_("beta"), CH), ALU.mult).then_inc(N["dve_rows"], 1)
                    V.tensor_copy(T[:, :, :], rep(c("eye"), 8))
                    V.tensor_copy(TT[:, :, :], rep(c("eye"), 8))
                    ch(tt(sm[:, 16:24], s_("beta"), s_("eg"), ALU.mult))
                if s == 1:
                    dve.wait_ge(N["act_sqk"], 1 + j + 1)
                    dve.wait_ge(N["pe_w"], 1 + 2 * j)
                    ch(V.tensor_reduce(sm[:, 0:8], u8, X, ALU.add))
                    ch(ts(sm[:, 0:8], sm[:, 0:8], RMS_EPS, ALU.add))
                    rsqrt(ch, sm[:, 48:56], sm[:, 0:8])
                    for t in range(TOK):
                        last = tt(kn[:, t], B4[1 + t], bc(sm[:, 48 + 4 * t:52 + 4 * t], P), ALU.mult)
                    last.then_inc(N["dve_kn"], 1)
                    dve.wait_ge(N["dve_kn"], 1 + j + 1)
                    dve.wait_ge(N["pe_b"], 1 + 4 * j)
                    ch(tt(ktail8, kn8, bc(s_("tail"), P), ALU.mult))
                if s == 2:
                    dve.wait_ge(N["act_decay"], 1 + j + 1)
                    ch(tt(decm[:, :, :], decm[:, :, :], rep(c("incl"), 8), ALU.mult))
                    dve.wait_ge(N["pe_qss"], 1 + j + 1)
                    ts(sm[:, 56:64], B[3][:, 0:8], RMS_EPS, ALU.add, float(P), ALU.mult).then_inc(N["dve_rq"], 1)
                    dve.wait_ge(N["dve_rq"], 1 + j + 1)
                    rsqrt(ch, sm[:, 0:8], sm[:, 56:64])
                    ch(tt(sm[:, 8:16], sm[:, 0:8], sm[:, 0:8], ALU.mult))
                if s == 4:
                    dve.wait_ge(evac[1], 2 * j + 2)
                    ch(tt(zs8, zs8, rep(par[:, slice(*PARAM["dnw"])], 8), ALU.mult))
                if s == 5:
                    dve.wait_ge(N["pe_kq"], 1 + j + 1)
                    ch(tt(AT[:, :, :], B8[1], decm[:, :, :], ALU.mult))
                    ch(tt(QKT[:, :, :], B8[2], decm[:, :, :], ALU.mult))
                if s == 6:
                    dve.wait_ge(N["act_br"], 1 + j + 1)
                    tt(AT[:, :, :], AT[:, :, :], TTg[:, :, :], ALU.mult).then_inc(N["dve_at"], 1)
                if 7 <= s < 7 + 2 * LEVELS:
                    lv, odd = divmod(s - 7, 2)
                    a0 = CONST["level"][0] + lv * CH
                    if not odd:
                        dve.wait_ge(N["pe_p"], 1 + LEVELS * j + lv + 1)
                        tt(Pm[:, :, :], B8[1], rep(cst[:, a0:a0 + CH], 8), ALU.mult).then_inc(N["dve_p"], 1)
                    else:
                        dve.wait_ge(N["pe_t"], 1 + LEVELS * j + lv + 1)
                        ins = tt(TT[:, :, :], TT[:, :, :], B8[2], ALU.subtract)
                        if lv < LEVELS - 1:
                            ins = tt(T[:, :, :], T[:, :, :], B8[3], ALU.subtract)
                        ins.then_inc(N["dve_t"], 1)
                if s == 18:
                    dve.wait_ge(N["dve_t"], 1 + LEVELS * (j + 1))
                    tt(TTb[:, :, :], TT[:, :, :], bc(s_("beta"), CH), ALU.mult)
                    tt(TTg[:, :, :], TT[:, :, :], bc(sm[:, 16:24], CH), ALU.mult).then_inc(N["dve_tb"], 1)
                if s == 20:
                    dve.wait_ge(N["pe_a"], 1 + 4 * j)
                    V.memset(S[:, :, :], 0.0).then_inc(N["dve_s"], 1)
                if 21 <= s < 29:
                    ck, odd = divmod(s - 21, 2)
                    t, p = divmod(ck, 2)
                    a = slice(p * CH, (p + 1) * CH)
                    if not odd:
                        dve.wait_ge(N["pe_a"], 1 + 4 * j + ck + 1)
                        dve.wait_ge(N["act_u"], 1 + j + 1)
                        tt(vn[a], u_sq[a, t], B4[1][a], ALU.subtract).then_inc(N["dve_vn"], 1)
                        if ck < 3:
                            t0 = SC["total"][0] + 4 * ck
                            ch(tt(S[:, :, :], S[:, :, :], bc(cur[:, t0:t0 + 4], P), ALU.mult))
                    else:
                        dve.wait_ge(N["pe_b"], 1 + 4 * j + ck + 1)
                        if ck < 3:
                            tt(S[:, :, :], S[:, :, :], B4[1], ALU.add).then_inc(N["dve_s"], 1)
                        if p:
                            e0 = SC["eg"][0] + 4 * t
                            tt(knT_o[:, t], B4[2], bc(cur[:, e0:e0 + 4], P), ALU.mult).then_inc(N["dve_o1"], 1)
                            dve.wait_ge(N["dve_o1"], 1 + 2 * j + t + 1)
                            tt(knT_o[:, t], knT_o[:, t], B4[3], ALU.add).then_inc(N["dve_o2"], 1)
                if s in (26, 30):
                    t = (s - 26) // 4
                    q4 = slice(4 * t, 4 * t + 4)
                    dve.wait_ge(N["act_osq"], 1 + 2 * j + t + 1)
                    ch(V.tensor_reduce(sm[:, 24:28], kn[:, t], X, ALU.add))
                    ch(stt(sm[:, 24:28], sm[:, 24:28], 1.0 / P, sm[:, 8 + 4 * t:12 + 4 * t], ALU.mult, ALU.mult))
                    ch(ts(sm[:, 24:28], sm[:, 24:28], RMS_EPS, ALU.add))
                    rsqrt(ch, sm[:, 48:52], sm[:, 24:28])
                    ch(tt(sm[:, 24:28], sm[:, 48:52], sm[:, q4], ALU.mult))
                    ch(tt(knT_o[:, t], knT_o[:, t], bc(sm[:, 24:28], P), ALU.mult))
                    tt(knT_o[:, t], knT_o[:, t], zs[:, t, :].rearrange("p (h d) -> p h d", h=HB), ALU.mult
                       ).then_inc(N["dve_oh"], 1)
                if s in (29, 31):
                    t = (s - 29) // 2
                    dve.wait_ge(N["act_oT"], 1 + 2 * j + t + 1)
                    tt(lo(act_a, HB * j, HB, t * P, (t + 1) * P), B4[1 + t], hi(act_a, HB * j, HB, t * P, (t + 1) * P),
                       ALU.subtract).then_inc(N["dve_oT"], 1)

            def body(n, mixes=()):
                for s in range(BODY):
                    split(n, s)
                    for mix in mixes:
                        mix(s)

            def chained(name, base, fn, j, links, slots=BODY):
                ch = Chain(dve, N[name], 1 + base)
                def run(s):
                    fn(j, s, ch)
                    if s == slots - 1:
                        assert ch.n == links, (name, ch.n)
                return run

            body(0, [lambda s: dn_conv(0, s)])
            with dve.Fori(1, NB) as j:
                body(BODY * j, [chained("dn_chain", DN_LINKS * (j - 1), dn_mix, j - 1, DN_LINKS),
                                lambda s: dn_conv(j, s)])

            def da_mix(j, s, ch):
                h, step = divmod(s, 4)
                if s == 0:
                    a0 = CONST["slopes"][0]
                    ch(V.tensor_copy(sm[:, 44:48].unsqueeze(1), cst[:, a0:a0 + HEADS].rearrange(
                        "p (j h) -> p j h", j=NB)[:, bass.ds(j, 1), :]))
                if h < HB and step == 0:
                    dve.wait_ge(N["pe_s"], 1 + HB * j + h + 1)
                    dve.wait_ge(N["act_oss"], 1 + HB * j + h)
                    for m in range(2):
                        ins = stt(pr[:, m, :], c("negdist"), sm[:, 44 + h:45 + h], B[1 + m][:, 0:3 * P],
                                  ALU.mult, ALU.add)
                    ins.then_inc(N["dve_s1"], 1)
                    dve.wait_ge(N["dve_s1"], 1 + HB * j + h + 1)
                    V.tensor_reduce(sm[:, 24:26], pr[:, :, 0:P], X, ALU.max)
                    ch(V.tensor_reduce(sm[:, 26:28], pr[:, :, P:3 * P], X, ALU.max))
                    ts(sm[:, 28:32], sm[:, 24:28], -1.0, ALU.mult).then_inc(N["dve_mx"], 1)
                if h < HB and step == 1:
                    dve.wait_ge(N["act_exp"], 1 + HB * j + h + 1)
                    ch(V.reciprocal(sm[:, 36:40], sm[:, 32:36]))
                    ch(ts(sm[:, 37:40:2], sm[:, 37:40:2], lam[:, 0:1], ALU.mult))
                    for r, (a, b) in enumerate([(0, P), (P, 3 * P)]):
                        ins = ts(pr[:, 1, a:b], pr[:, 1, a:b], sm[:, 37 + 2 * r:38 + 2 * r], ALU.mult)
                    ch(ins)
                    for r, (a, b) in enumerate([(0, P), (P, 3 * P)]):
                        ins = stt(pr[:, 0, a:b], pr[:, 0, a:b], sm[:, 36 + 2 * r:37 + 2 * r], pr[:, 1, a:b],
                                  ALU.mult, ALU.subtract)
                    ins.then_inc(N["dve_pd"], 1)
                if h < HB and step == 3:
                    dve.wait_ge(N["act_oss"], 1 + HB * j + h + 1)
                    dve.wait_ge(N["pe_oT2"], 1 + HB * j + h)
                    ch(ts(sm[:, 42:44], sm[:, 40:42], 1.0 / P, ALU.mult, RMS_EPS, ALU.add))
                    rsqrt(ch, sm[:, 48:50], sm[:, 42:44])
                    ch(tt(oh[:, :, :], B[3][:, 0:SEQ].rearrange("p (t d) -> p t d", t=TOK), bc(sm[:, 48:50], P),
                          ALU.mult))
                    stt(oh[:, :, :], oh[:, :, :], 1.0 - LAMBDA_INIT, rep(par[:, slice(*PARAM["daw"])], TOK),
                        ALU.mult, ALU.mult).then_inc(N["dve_oh2"], 1)
                h, step = divmod(s - 5, 4)
                if 0 <= h < HB and step == 0:
                    dve.wait_ge(N["act_oT2"], 1 + HB * j + h + 1)
                    tt(lo(act_b, HB * j + h, 1), B[0][:, 0:SEQ].unsqueeze(1), hi(act_b, HB * j + h, 1), ALU.subtract
                       ).then_inc(N["dve_oT2"], 1)

            body(N_DA, [chained("dn_chain", DN_LINKS * (NB - 1), dn_mix, NB - 1, DN_LINKS)])
            with dve.Fori(1, NB) as j:
                body(N_DA + BODY * j, [chained("da_chain", DA_LINKS * (j - 1), da_mix, j - 1, DA_LINKS)])
            body(N_GB, [chained("da_chain", DA_LINKS * (NB - 1), da_mix, NB - 1, DA_LINKS)])

            def turn_rows(cnt, place):
                buf, k = place
                for t in range(TOK):
                    dve.wait_ge(N["act_mT"], 1 + 2 * cnt + t + 1)
                    ins = tt(lo(buf, k, 4, t * P, (t + 1) * P), B4[t], hi(buf, k, 4, t * P, (t + 1) * P), ALU.subtract)
                ins.then_inc(N["dve_mT"], 1)

            def branch(n, j, turned):
                for s in range(2 * TPG):
                    split(n, s)
                    if s == 1 and turned:
                        turn_rows(j - 1, (act_x, 4 * (j - 1)))
                    if s == TPG - 1:
                        dve.wait_ge(tile_used, n + s + 1)
                        dve.wait_ge(N["pe_qkT"], 1 + 4 * NB)
                        dve.wait_ge(N["pe_mT"], 1 + j)
                        for t in range(TOK):
                            ins = tt(hraw[:, t, :], pg[0][t][:, :], gates[:, 0, t, bass.ds(NG * j, NG)], ALU.mult)
                        ins.then_inc(evac[0], 1)
                    if s == 2 * TPG - 1:
                        dve.wait_ge(tile_used, n + s + 1)
                        for t in range(TOK):
                            ins = tt(vda[:, t, :], pg[1][t][:, :], gates[:, 1, t, bass.ds(NG * j, NG)], ALU.mult)
                        ins.then_inc(evac[1], 1)
                        dve.wait_ge(evac[1], 4 * NB + 2 + j + 1)
                        tt(hraw[:, :, :], hraw[:, :, :], vda[:, :, :], ALU.add).then_inc(N["dve_m"], 1)

            branch(N_BR, 0, False)
            with dve.Fori(1, NB) as j:
                branch(N_BR + 2 * TPG * j, j, True)
            turn_rows(NB - 1, (act_x, 4 * (NB - 1)))
            for g in range(4):
                for q in range(TPG):
                    split(N_OUT, g * TPG + q)
                dve.wait_ge(tile_used, N_OUT + (g + 1) * TPG)
                dve.wait_ge(xres_full[g % 2], 16 * (g // 2 + 1))
                for t in range(TOK):
                    ins = stt(y[:, t, g * NG:(g + 1) * NG], xres[g % 2][:, t, :], ALPHA, pg[g % 2][t][:, :],
                              ALU.mult, ALU.add)
                ins.then_inc(evac[g % 2], 1)
                dve.wait_ge(evac[g % 2], 4 * NB + 2 + NB + g // 2 + 1)
                for t in range(TOK):
                    ins = V.bn_stats(lnst[:, t, g, :], y[:, t, g * NG:(g + 1) * NG])
                ins.then_inc(xres_used, 1)

            lnc = Chain(dve, N["ln_chain"])

            def layer_norm(i):
                for t in range(TOK):
                    lnc(V.bn_aggr(lnmv[:, t, :], lnst[:, t, :, :].rearrange("p g s -> p (g s)")))
                    lnc(ts(sm[:, 56 + t:57 + t], lnmv[:, t, 1:2], LN_EPS, ALU.add))
                    rsqrt(lnc, lnmv[:, t, 1:2], sm[:, 56 + t:57 + t])
                    stt(lnmv[:, t, 0:1], lnmv[:, t, 0:1], -1.0, lnmv[:, t, 1:2], ALU.mult, ALU.mult
                        ).then_inc(N["act_var"], 1)
                dve.wait_ge(ln_full, 16 * (i + 1))
                for t in range(TOK):
                    dve.wait_ge(N["dve_xc"], 2 * i + t + 1)
                    lnc(tt(y[:, t, :], y[:, t, :], lnp[:, 0, :], ALU.mult))
                    tt(y[:, t, :], y[:, t, :], lnp[:, 1, :], ALU.add).then_inc(N["dve_x1" if i == 0 else "dve_out"], 1)

            dve.wait_ge(xres_used, 4)
            layer_norm(0)
            for i in range(8):
                t, cq = divmod(i, 4)
                dve.wait_ge(N["act_x1T"], i + 1)
                tt(act_a[:, 1, 4 * cq:4 * cq + 4, t * P:(t + 1) * P], B4[i % 4],
                   act_a[:, 0, 4 * cq:4 * cq + 4, t * P:(t + 1) * P], ALU.subtract).then_inc(N["dve_x1T"], 1)

            def up(n, g, cnt, place):
                for s in range(2 * TPG):
                    split(n, s)
                    if s == 1 and place:
                        turn_rows(cnt - 1, place)
                dve.wait_ge(tile_used, n + 2 * TPG)
                dve.wait_ge(evac[0], g + 1)
                dve.wait_ge(N["pe_mT"], 1 + cnt)
                for t in range(TOK):
                    ins = tt(hraw[:, t, :], pg[1][t][:, :], vda[:, t, :], ALU.mult)
                ins.then_inc(N["dve_m"], 1)
                dve.wait_ge(N["dve_m"], 1 + cnt + 1)
                dve.sem_inc(evac[1], 1)

            def down_half(piece, n, g, i, tiles):
                for e in range(2):
                    for q in range(tiles):
                        split(n + 2 * tiles * i, e * tiles + q)
                    dve.wait_ge(tile_used, n + 2 * tiles * i + (e + 1) * tiles)
                    for t in range(TOK):
                        yv = y[:, t, bass.ds(2 * NG * i + NG * e, NG)]
                        ins = stt(yv, yv, ALPHA if piece == 0 else 1.0, pg[e][t][:, :], ALU.mult, ALU.add)
                    ins.then_inc(evac[e], 1)
                    if piece == 2:
                        dve.wait_ge(evac[e], g + i + 1)
                        for t in range(TOK):
                            ins = V.bn_stats(lnst[:, t, 2 * i + e, :], y[:, t, bass.ds(2 * NG * i + NG * e, NG)])
                        lnc(ins)

            def down(piece, n, g, tiles, buf):
                if piece < 2:
                    with dve.Fori(0, 2) as i:
                        down_half(piece, n, g, i, tiles)
                else:
                    for i in range(2):
                        down_half(piece, n, g, i, tiles)

            ffn_walk(dve, up, down, lambda cnt, place: turn_rows(cnt - 1, place))
            layer_norm(1)


def _constants():
    i = np.arange(P)
    same = (i[:, None] // CH == i[None, :] // CH)
    cc = np.arange(CH)
    ic = i % CH
    out = np.zeros((P, NCONST), np.float32)

    def put(name, a):
        out[:, slice(*CONST[name])] = a
    put("ident", np.eye(P))
    put("after", same & (i[:, None] > i[None, :]))
    put("same", same)
    put("upto", ic[:, None] <= cc[None, :])
    put("eye", ic[:, None] == cc[None, :])
    put("incl", cc[None, :] >= ic[:, None])
    lv = []
    for b in range(LEVELS):
        w = 1 << b
        lv.append((ic[:, None] // (2 * w) == cc[None, :] // (2 * w)) & (ic[:, None] // w % 2 == 1) & (cc[None, :] // w % 2 == 0))
    put("level", np.concatenate(lv, 1))
    d0 = (i[:, None] - i[None, :]).astype(np.float32)
    d1 = (P + i[:, None] - np.arange(SEQ)[None, :]).astype(np.float32)
    put("negdist", np.concatenate([np.where(d >= 0, -d, np.float32(-1e30)) for d in (d0, d1)], 1))
    put("slopes", np.broadcast_to(np.exp2(-8.0 * np.arange(1, HEADS + 1) / HEADS), (P, HEADS)))
    early = np.concatenate([same & (i[:, None] <= i[None, :]), np.broadcast_to(i[:, None] < CH, (P, P)),
                            np.broadcast_to(i[:, None] >= CH, (P, P))], 1).astype(np.float32)
    return out, early


def _tiles(w):
    k, n = w.shape
    return w.reshape(k // (TK * P), TK, P, n // NG, NG).transpose(3, 0, 2, 1, 4).reshape(n // NG, k // (TK * P), P, TK * NG)


def kernel(**inputs):
    import concourse.bacc as bacc
    from concourse.bass_utils import run_bass_kernel_spmd

    a = {k: np.asarray(v) for k, v in inputs.items()}
    x = a["x"][0]
    w = a["w_in"][0]
    qkv = HEADS * P
    at = {"q": 0, "k": qkv, "v": 2 * qkv, "z": 3 * qkv}
    ab = w[:, 4 * qkv:4 * qkv + 2 * HEADS]
    o = 4 * qkv + 2 * HEADS
    at.update({"aq": o, "ak": o + qkv, "av": o + 2 * qkv, "ga": o + 3 * qkv, "gb": o + 3 * qkv + D})
    order = [(n, j) for j in range(NB) for n in ("k", "v", "q", "z")]
    order += [(n, 0) for n in ("aq", "ak", "av", "ga")]
    order += [(n, j) for j in range(1, NB) for n in ("ga", "aq", "ak", "av")]
    order += [("gb", j) for j in range(NB)]
    stream = [_tiles(w[:, at[n] + NG * j:at[n] + NG * (j + 1)])[0] for n, j in order]
    wa, wb, wo = (_tiles(a[n][0]) for n in ("w_branch_a", "w_branch_b", "w_out"))
    for j in range(NB):
        stream += [wa[j], wb[j]]
    stream += [wo[j] for j in range(4)]
    wg, wu, wd = (_tiles(a[n][0]) for n in ("w_gate", "w_up", "w_down"))

    def ups(f0, f1):
        for f in range(f0, f1):
            stream.append(wg[f])
            stream.append(wu[f])

    def down(p):
        f0, f1 = PIECES[p]
        for g in range(4):
            stream.append(wd[g][2 * f0:2 * f1])
    ups(0, 5)
    down(0)
    ups(5, 9)
    down(1)
    ups(9, FG)
    down(2)
    weights = np.concatenate(stream, 0)
    consts, early = _constants()

    def wide(v):
        return np.broadcast_to(v.reshape(1, -1), (P, v.size))
    cv = a["conv_w"][0].reshape(CONV, 3, NB, HB, P)[:, [1, 2, 0]]
    params = np.concatenate([cv.transpose(4, 2, 1, 3, 0).reshape(P, -1), wide(a["dn_norm_w"][0]),
                             wide(a["da_norm_w"][0]), wide(a["dt_bias"][0]), wide(a["a_log"][0])], 1)
    ln_in = np.stack([np.broadcast_to(np.stack([a["ln_g"][0, i], a["ln_b"][0, i]]), (P, 2, D)) for i in range(2)])
    data = {
        "xT": x.T.reshape(4, 4, P, SEQ).transpose(0, 2, 1, 3),
        "xrow": x.reshape(TOK, P, 4, NG).transpose(2, 1, 0, 3),
        "weights": weights,
        "w_ab": ab.reshape(KC, P, 2 * HEADS).transpose(1, 0, 2).reshape(P, -1),
        "consts": consts, "early": early, "params": params, "lam_in": wide(a["da_lambda"][0]), "ln_in": ln_in,
    }
    nc = bacc.Bacc("TRN2", target_bir_lowering=False, num_devices=1)
    arrays, aps = {}, []
    for name, v in data.items():
        arrays["in_" + name] = np.ascontiguousarray(v)
        aps.append(nc.dram_tensor("in_" + name, v.shape, mybir.dt.from_np(v.dtype), kind="ExternalInput").ap())
    aps.append(nc.dram_tensor("out", (1, SEQ, D), F32, kind="ExternalOutput").ap())
    build(nc, *aps)
    r = run_bass_kernel_spmd(nc, [arrays], core_ids=[0])
    return r.results[0]["out"]
```

```python
import math
from contextlib import ExitStack

import numpy as np

import concourse.bass as bass
from concourse import mybir

F32 = mybir.dt.float32
I32 = mybir.dt.int32
F32R = mybir.dt.float32r
ALU = mybir.AluOpType
ACT = mybir.ActivationFunctionType
X = mybir.AxisListType.X

P = 128
D = 2048
SEQ = 256
TOK = SEQ // P
KC = D // P
HEADS = 16
HB = 4
NB = HEADS // HB
CH = 64
CONV = 4
D_FF = -(-8 * D // (3 * 256)) * 256
NG = 512
TK = 2
CONV_SLOTS = [(9, 12), (17, 20), (25, 27)]
DA_TURN = [(21, 23), (27, 29)]
DA_TURN_FIRST = [(10, 12), (18, 20)]
HEAD_SLOTS = [0, 6, 12, 18]
CK_SLOTS = [18, 20, 23, 25]
CONV_LINKS, DN_LINKS, DA_LINKS = 12, 56, 69
TPG = KC // TK
RING = 4
AHEAD = 3
ALPHA = 2.0 ** 0.25
LAMBDA_INIT = 0.8 - 0.6 * math.exp(0.0)
LN_EPS = 1e-5
RMS_EPS = 1e-6
FG = D_FF // NG
PIECES = [(0, 4), (4, 8), (8, FG)]
BODY = 4 * TPG

N_DN, N_DA = 0, NB * BODY
N_GB = N_DA + NB * BODY
N_BR = N_GB + BODY
N_OUT = N_BR + 2 * BODY
N_FFN = N_OUT + BODY
N_TILES = N_FFN + 2 * TPG * FG + 4 * (D_FF // P // TK)
LEVELS = 6

CONST = {}
_at = 0
for _n, _w in [("ident", P), ("after", P), ("same", P), ("upto", CH), ("eye", CH), ("incl", CH),
               ("pairs", CH), ("level", LEVELS * CH), ("negdist", 3 * P), ("slopes", HEADS)]:
    CONST[_n] = (_at, _at + _w)
    _at += _w
NCONST = _at
PARAM = {}
_at = 0
for _n, _w in [("conv", NB * 3 * HB * CONV), ("dnw", P), ("daw", P), ("dt", HEADS), ("alog", HEADS)]:
    PARAM[_n] = (_at, _at + _w)
    _at += _w
NPARAM = _at
SC = {"beta": (0, 8), "g": (8, 16), "eg": (16, 24), "tail": (24, 32), "total": (32, 48)}
NSC = 48


def build(nc, xT, xrow, weights, w_ab, consts, early, params, lam_in, ln_in, out):
    ctx = ExitStack()

    def sb(name, shape, dt=F32):
        return ctx.enter_context(nc.sbuf_tensor(name, shape, dt))

    def sem(name):
        return ctx.enter_context(nc.semaphore(name))

    with ctx:
        act_x = sb("act_x", [P, 2, KC, SEQ], F32R)
        act_a = sb("act_a", [P, 2, KC, SEQ], F32R)
        dn = ExitStack()

        def tmp(name, shape):
            return dn.enter_context(nc.sbuf_tensor(name, shape, F32))

        cT = tmp("cT", [P, 3, HB, SEQ])
        kn = tmp("kn", [P, 2, HB, P])
        ktail = tmp("ktail", [P, 2, HB, P])
        vtok = tmp("vtok", [P, 2, HB, P])
        knT_o = tmp("knT_o", [P, 2, HB, P])
        u_sq = tmp("u_sq", [P, 2, HB, P])
        w_sq = tmp("w_sq", [P, 2 * HB * P])
        decm = tmp("decm", [P, 8, CH])
        AT = tmp("AT", [P, 8, CH])
        QKT = tmp("QKT", [P, 8, CH])
        T = tmp("T", [P, 8, CH])
        TT = tmp("TT", [P, 8, CH])
        Pm = tmp("Pm", [P, 8, CH])
        TTb = tmp("TTb", [P, 8, CH])
        TTg = tmp("TTg", [P, 8, CH])
        S = tmp("S", [P, HB, P])
        vn = tmp("vn", [P, HB, P])
        zs = tmp("zs", [P, 2, NG])
        dn.close()
        act_b = sb("act_b", [P, 2, KC, SEQ], F32R)
        gates = sb("gates", [P, 2, TOK, D])
        y = gates[:, 0]
        lnp = gates[:, 1]

        raw = sb("raw", [P, RING, TK, NG])
        whi = sb("whi", [P, RING, TK, NG], F32R)
        wlo = sb("wlo", [P, RING, TK, NG], F32R)
        cst = sb("cst", [P, NCONST])
        par = sb("par", [P, NPARAM])
        scal = sb("scal", [P, NB, NSC])
        cur = sb("cur", [P, NSC])
        cw = sb("cw", [P, 3, HB, CONV])
        sm = sb("sm", [P, 72])
        lam = sb("lam", [P, 2])
        g_all = sb("g_all", [P, TOK * HEADS])
        pz = sb("pz", [P, 4, TOK * HEADS])
        lnst = sb("lnst", [P, TOK, 4, 6])
        lnmv = sb("lnmv", [P, TOK, 2])
        hraw = sb("hraw", [P, TOK, NG])
        qT = sb("qT", [P, HB, SEQ])
        kT = sb("kT", [P, HB, SEQ])
        vda = sb("vda", [P, TOK, NG])
        pr = sb("pr", [P, 2, 3 * P])
        pT = sb("pT", [P, 3 * P])
        oh = sb("oh", [P, TOK, P])

        pg = [[ctx.enter_context(nc.psum_tensor(f"pg{a}{t}", [P, NG], F32)) for t in range(TOK)] for a in range(2)]
        B = [ctx.enter_context(nc.psum_tensor(f"B{i}", [P, NG], F32)) for i in range(4)]

        def c(name):
            a, b = CONST[name]
            return cst[:, a:b]

        def s_(name):
            a, b = SC[name]
            return cur[:, a:b]

        ident = c("ident")
        B4 = [b[:, :].rearrange("p (h d) -> p h d", h=HB) for b in B]
        B8 = [b[:, :].rearrange("p (h d) -> p h d", h=8) for b in B]

        def bc(ap, n):
            return ap.unsqueeze(2).broadcast_to([P, ap.shape[1], n])

        def rep(ap, m):
            return ap.unsqueeze(1).broadcast_to([P, m, ap.shape[1]])

        xt4 = [cT[:, 0], cT[:, 1], cT[:, 2],
               kn[:, :, :, :].rearrange("p t h d -> p (t h d)").rearrange("p (h s) -> p h s", h=HB)]
        xres = [b[:, :, :].rearrange("p h s -> p (h s)").rearrange("p (t n) -> p t n", t=TOK) for b in (qT, kT)]
        upto_r, sel0, sel1 = (u_sq[:, 0, i, :] for i in range(3))
        kn8, ktail8, u8, zs8 = (b.rearrange("p (i d) -> p i d", d=P) for b in (
            kn[:, :, :, :].rearrange("p t h d -> p (t h d)"), ktail[:, :, :, :].rearrange("p t h d -> p (t h d)"),
            u_sq[:, :, :, :].rearrange("p t h d -> p (t h d)"), zs[:, :, :].rearrange("p t n -> p (t n)")))

        raw_full = [sem(f"raw_full{i}") for i in range(RING)]
        hi_done = sem("hi_done")
        lo_done = sem("lo_done")
        tile_used = sem("tile_used")
        evac = [sem("evac_even"), sem("evac_odd")]
        xt_full = [sem(f"xt_full{i}") for i in range(4)]
        const_full = sem("const_full")
        ln_full = sem("ln_full")
        xres_full = [sem("xres_full0"), sem("xres_full1")]
        xres_used = sem("xres_used")
        out_full = sem("out_full")
        x_hi = sem("x_hi")
        x_lo = sem("x_lo")
        once = """pe_passed pe_ab pe_sc0 act_pro dve_pro dve_sc0 act_tot dve_lam act_lam
            dve_x1 pe_x1T act_x1T dve_x1T act_var act_xn pro_chain ln_chain""".split()
        counted = """pe_conv dve_conv act_silu dve_cw act_tap
            pe_ktok pe_dt pe_qss pe_v pe_knT pe_kq pe_br pe_p pe_t pe_u pe_w pe_a pe_b pe_oT
            act_sqk act_sqq act_decay act_v act_knT act_br act_u act_w act_osq act_oT
            dve_rows dve_kn dve_rq dve_at dve_p dve_t dve_tb dve_s dve_vn dve_o1 dve_o2 dve_oh dve_oT0 dve_oT
            pe_qkT act_qkT pe_s dve_s1 dve_mx act_exp dve_pd pe_pT act_pT pe_pv act_oss dve_oh2 pe_oT2
            act_oT2 dve_oT2 dve_m pe_mT act_mT dve_mT conv_chain dn_chain da_chain""".split()
        N = {n: sem(n) for n in once + counted}

        class Chain:

            def __init__(self, eng, sm_, base=0):
                self.eng, self.sem, self.base, self.n = eng, sm_, base, 0

            def __call__(self, ins):
                self.n += 1
                ins.then_inc(self.sem, 1)
                self.eng.wait_ge(self.sem, self.base + self.n)

        def hi(buf, k, n, t0=0, t1=SEQ):
            return buf[:, 0, bass.ds(k, n), t0:t1]

        def lo(buf, k, n, t0=0, t1=SEQ):
            return buf[:, 1, bass.ds(k, n), t0:t1]


        def ffn_walk(eng, up, down):
            n, g, cnt = N_FFN, 4 * NB + 2 + NB + 2, NB
            up(n, g, cnt, None)
            with eng.Fori(1, 4) as f:
                up(n + 2 * TPG * f, g + f, cnt + f, (act_x, 4 * (f - 1)))
            up(n + 2 * TPG * 4, g + 4, cnt + 4, (act_x, 12))
            n, g, cnt = n + 2 * TPG * 5, g + 5, cnt + 5
            down(0, n, g, TPG, act_x, cnt, (act_b, 0))
            n, g = n + 4 * TPG, g + 2
            up(n, g, cnt, None)
            with eng.Fori(1, 3) as f:
                up(n + 2 * TPG * f, g + f, cnt + f, (act_b, 4 * f))
            up(n + 2 * TPG * 3, g + 3, cnt + 3, (act_b, 12))
            n, g, cnt = n + 2 * TPG * 4, g + 4, cnt + 4
            down(1, n, g, TPG, act_b, cnt, (act_x, 0))
            n, g = n + 4 * TPG, g + 2
            up(n, g, cnt, None)
            up(n + 2 * TPG, g + 1, cnt + 1, (act_x, 4))
            n, g, cnt = n + 4 * TPG, g + 2, cnt + 2
            down(2, n, g, 2 * (FG - 8), act_x, cnt, (act_x, 8))

        block = ctx.enter_context(nc.Block())

        @block.sync
        def _(sp):
            for i in range(4):
                sp.dma_start(xt4[i], xT[i]).then_inc(xt_full[i], 16)
                sp.dma_start(raw[:, i].rearrange("p k n -> p (k n)"), weights[i]).then_inc(raw_full[i], 16)
            sp.dma_start(w_sq[:, 0:NG], w_ab).then_inc(const_full, 16)
            sp.dma_start(cst[:, :], consts).then_inc(const_full, 16)
            sp.dma_start(par[:, :], params).then_inc(const_full, 16)
            sp.dma_start(u_sq[:, 0, 0:3, :].rearrange("p a b -> p (a b)"), early).then_inc(const_full, 16)
            sp.dma_start(vda[:, 0, 0:4 * CH], lam_in).then_inc(const_full, 16)
            total = weights.shape[0]
            for n in counted:
                sp.sem_inc(N[n], 1)

            def later(m):
                for r in range(RING):
                    sp.wait_ge(hi_done, RING * m + r - RING + 1)
                    sp.wait_ge(lo_done, RING * m + r - RING + 1)
                    sp.dma_start(raw[:, r].rearrange("p k n -> p (k n)"),
                                 weights[bass.ds(RING * m + r, 1)].rearrange("o p n -> (o p) n")
                                 ).then_inc(raw_full[r], 16)
            out_m = N_OUT // RING
            with sp.Fori(1, out_m) as m:
                later(m)
            sp.wait_ge(N["dve_oT2"], 1 + HEADS)
            for g in range(2):
                sp.dma_start(xres[g], xrow[g]).then_inc(xres_full[g], 16)
            for i in range(6):
                later(out_m + i)
                if i == 1:
                    sp.wait_ge(N["dve_m"], 1 + NB)
                if 1 <= i < 5:
                    a = slice((i - 1) * NG, i * NG)
                    sp.dma_start(lnp[:, :, a], ln_in[0, :, :, a]).then_inc(ln_full, 16)
                if i in (3, 5):
                    g = (i + 1) // 2
                    sp.wait_ge(xres_used, g - 1)
                    sp.dma_start(xres[g % 2], xrow[g]).then_inc(xres_full[g % 2], 16)
            at = out_m + 6
            with sp.Fori(at, total // RING) as m:
                later(m)
            sp.wait_ge(N["dve_x1"], 8)
            sp.dma_start(lnp, ln_in[1]).then_inc(ln_full, 16)
            for i in range(8):
                cq, t = divmod(i, TOK)
                sp.wait_ge(N["dve_x1"], 8 + i + 1)
                sp.dma_start(out[0, t * P:(t + 1) * P, cq * NG:(cq + 1) * NG], y[:, t, cq * NG:(cq + 1) * NG]
                             ).then_inc(out_full, 16)
            sp.wait_ge(out_full, 16 * 8)


        @block.tensor
        def _(pe):
            def mm(o, l, r, start=True, stop=True):
                return nc.tensor.matmul(o, l, r, start=start, stop=stop)

            def gemm_tile(n, q, a, k0, pair, last):
                r = q % RING
                pe.wait_ge(hi_done, n + 1)
                pe.wait_ge(lo_done, n + 1)
                for k in range(TK):
                    for t in range(TOK):
                        xh = a[:, 0, k0 + k, t * P:(t + 1) * P]
                        xl = a[:, 1, k0 + k, t * P:(t + 1) * P]
                        first = k0 + k == 0
                        mm(pg[pair][t][:, :], xh, whi[:, r, k, :], first, False)
                        mm(pg[pair][t][:, :], xh, wlo[:, r, k, :], False, False)
                        end = mm(pg[pair][t][:, :], xl, whi[:, r, k, :], False, last and k == TK - 1)
                end.then_inc(tile_used, 1)

            def prologue(s):
                if s == 2:
                    pe.wait_ge(const_full, 80)
                    for t in range(TOK):
                        for k in range(KC):
                            last = mm(B[t][:, 0:32], xt4[k // 4][:, k % 4, t * P:(t + 1) * P],
                                      w_sq[:, 32 * k:32 * k + 32], k == 0, k == KC - 1)
                    last.then_inc(N["pe_ab"], 1)
                if s == 6:
                    pe.wait_ge(N["dve_pro"], 1)
                    mm(B[2][:, 0:32], upto_r, g_all[:, :])
                    mm(B[2][:, 32:64], c("after"), g_all[:, :])
                    mm(B[2][:, 64:96], sel0, g_all[:, :])
                    mm(B[2][:, 96:128], sel1, g_all[:, :]).then_inc(N["pe_sc0"], 1)

            def x_ready(s):
                if s < TPG and s % 2 == 0:
                    pe.wait_ge(x_hi, s // 2 + 1)
                    pe.wait_ge(x_lo, s // 2 + 1)

            def turn_conv(j, kind, half):
                pe.wait_ge(evac[[0, 1, 0][kind]], 2 * j + [1, 1, 2][kind])
                pe.wait_ge(N["dve_conv"], 1 + 6 * j + 2 * kind + half)
                if kind == half == 0 and not isinstance(j, int):
                    pe.wait_ge(N["dve_oT"], j)
                for i in range(2):
                    for t in range(TOK):
                        h = 2 * half + i
                        last = nc.tensor.transpose(B[0][:, i * SEQ + t * P:i * SEQ + (t + 1) * P],
                                                   hraw[:, t, h * P:(h + 1) * P], ident)
                last.then_inc(N["pe_conv"], 1)

            def dn_conv(j, s):
                for kind, slots in enumerate(CONV_SLOTS):
                    if s in slots:
                        turn_conv(j, kind, slots.index(s))

            def waits_end():
                pe.sem_inc(N["pe_passed"], 1)

            def dn_mix(j, s):
                if s == 0:
                    pe.wait_ge(N["act_silu"], 1 + 3 * j + 1)
                    pe.wait_ge(N["dve_o2"], 1 + 2 * j)
                    for t in range(TOK):
                        for h in range(HB):
                            last = nc.tensor.transpose(B4[1 + t][:, h, :], cT[:, 0, h, t * P:(t + 1) * P], ident)
                    last.then_inc(N["pe_ktok"], 1)
                if s == 1:
                    pe.wait_ge(N["dve_rows"], 1 + j + 1)
                    pe.wait_ge(N["dve_oT0"], 1 + j)
                    mm(B[3][:, :], c("after"), Pm[:, :, :].rearrange("p a b -> p (a b)")).then_inc(N["pe_dt"], 1)
                if s == 2:
                    pe.wait_ge(N["act_decay"], 1 + j + 1)
                    pe.wait_ge(N["act_sqq"], 1 + j + 1)
                    for t in range(TOK):
                        for h in range(HB):
                            last = mm(B[3][:, 4 * t + h:4 * t + h + 1],
                                      w_sq[:, h * SEQ + t * P:h * SEQ + (t + 1) * P], c("incl")[:, CH - 1:CH])
                    last.then_inc(N["pe_qss"], 1)
                if s in (3, 4):
                    t = s - 3
                    if t == 0:
                        pe.wait_ge(N["act_silu"], 1 + 3 * j + 2)
                        pe.wait_ge(N["dve_rq"], 1 + j + 1)
                    else:
                        pe.wait_ge(N["act_v"], 1 + 2 * j + 1)
                    for h in range(HB):
                        last = nc.tensor.transpose(B4[3][:, h, :], cT[:, 1, h, t * P:(t + 1) * P], ident)
                    last.then_inc(N["pe_v"], 1)
                if s == 3:
                    pe.wait_ge(N["dve_kn"], 1 + j + 1)
                    for t in range(TOK):
                        for h in range(HB):
                            last = nc.tensor.transpose(B4[1 + t][:, h, :], kn[:, t, h, :], ident)
                    last.then_inc(N["pe_knT"], 1)
                if s == 5:
                    pe.wait_ge(N["act_knT"], 1 + j + 1)
                    for t in range(TOK):
                        for h in range(HB):
                            for p in range(2):
                                kc = knT_o[:, t, h, p * CH:(p + 1) * CH]
                                qc = cT[:, 2, h, t * P + p * CH:t * P + (p + 1) * CH]
                                mm(B8[1][p * CH:(p + 1) * CH, 4 * t + h, :], kc, kc)
                                last = mm(B8[2][p * CH:(p + 1) * CH, 4 * t + h, :], kc, qc)
                    last.then_inc(N["pe_kq"], 1)
                if s == 6:
                    pe.wait_ge(N["act_v"], 1 + 2 * j + 2)
                    mm(B[3][:, :], c("same"), TTb[:, :, :].rearrange("p a b -> p (a b)")).then_inc(N["pe_br"], 1)
                if s == 7:
                    pe.wait_ge(N["dve_at"], 1 + j + 1)
                    waits_end()
                    for i in range(8):
                        for p in range(2):
                            a = slice(p * CH, (p + 1) * CH)
                            last = mm(B8[1][a, i, :], AT[a, i, :], c("eye")[a])
                    last.then_inc(N["pe_p"], 1)
                if 8 <= s < 8 + 2 * (LEVELS - 1):
                    lv, odd = divmod(s - 6, 2)
                    if not odd:
                        pe.wait_ge(N["dve_t"], 1 + LEVELS * j + lv)
                        waits_end()
                        for i in range(8):
                            for p in range(2):
                                a = slice(p * CH, (p + 1) * CH)
                                last = mm(B8[1][a, i, :], AT[a, i, :], T[a, i, :])
                        last.then_inc(N["pe_p"], 1)
                    else:
                        pe.wait_ge(N["dve_p"], 1 + (LEVELS - 1) * j + lv)
                        waits_end()
                        for i in range(8):
                            for p in range(2):
                                a = slice(p * CH, (p + 1) * CH)
                                last = mm(B8[2][a, i, :], Pm[a, i, :], TT[a, i, :])
                                if lv < LEVELS - 1:
                                    last = mm(B8[3][a, i, :], TT[a, i, :], Pm[a, i, :])
                        last.then_inc(N["pe_t"], 1)
                if s == 18:
                    pe.wait_ge(N["dve_tb"], 1 + j + 1)
                    waits_end()
                    for t in range(TOK):
                        for h in range(HB):
                            for p in range(2):
                                a = slice(p * CH, (p + 1) * CH)
                                last = mm(B4[1 + t][a, h, :], TTb[a, 4 * t + h, :], vtok[a, t, h, :])
                    last.then_inc(N["pe_u"], 1)
                if s in (18, 19):
                    p = s - 18
                    if p:
                        pe.wait_ge(N["act_w"], 1 + 2 * j + 1)
                    a = slice(p * CH, (p + 1) * CH)
                    for t in range(1 - p, TOK):
                        for h in range(HB):
                            last = mm(B8[3][:, 4 * t + h, :], kn[a, t, h, :], TTg[a, 4 * t + h, :])
                    last.then_inc(N["pe_w"], 1)
                for ck in range(4):
                    t, p = divmod(ck, 2)
                    a = slice(p * CH, (p + 1) * CH)
                    if s == CK_SLOTS[ck] and ck:
                        if ck == 1:
                            pe.wait_ge(N["act_w"], 1 + 2 * j + 2)
                        if ck == 2:
                            pe.wait_ge(N["dve_o1"], 1 + 2 * j + 1)
                        pe.wait_ge(N["dve_s"], 1 + 3 * j + ck)
                        for h in range(HB):
                            wv = w_sq[:, (p * 8 + 4 * t + h) * CH:(p * 8 + 4 * t + h + 1) * CH]
                            mm(B4[1][a, h, :], wv, S[:, h, :])
                            last = mm(B4[2][a, h, :], cT[:, 2, h, ck * CH:(ck + 1) * CH], S[:, h, :])
                        last.then_inc(N["pe_a"], 1)
                    if s == CK_SLOTS[ck] + 1:
                        if ck == 0:
                            pe.wait_ge(N["act_u"], 1 + j + 1)
                            pe.wait_ge(N["act_w"], 1 + 2 * j + 2)
                        else:
                            pe.wait_ge(N["dve_vn"], 1 + 3 * j + ck)
                        if ck == 2:
                            pe.wait_ge(N["dve_o2"], 1 + 2 * j + 1)
                        waits_end()
                        for h in range(HB):
                            v = vn[a, h, :] if ck else u_sq[a, 0, h, :]
                            last = mm(B4[3][a, h, :], QKT[a, 4 * t + h, :], v)
                            if ck < 3:
                                last = mm(B4[1][:, h, :], ktail[a, t, h, :], v)
                        last.then_inc(N["pe_b"], 1)
                if s == 31:
                    for t in range(TOK):
                        pe.wait_ge(N["dve_oh"], 1 + 2 * j + t + 1)
                        if t == 1:
                            if isinstance(j, int):
                                pe.wait_ge(N["act_qkT"], 1 + 4)
                            else:
                                pe.wait_ge(N["dve_conv"], 1 + 6 * j + 12)
                        for h in range(HB):
                            last = nc.tensor.transpose(B4[3 - 3 * t][:, h, :], knT_o[:, t, h, :], ident)
                        last.then_inc(N["pe_oT"], 1)

            def da_turn(j, which, half, e, first):
                pe.wait_ge(evac[e[0]], e[1])
                pe.wait_ge(N["act_qkT"], 1 + 4 * j + 2 * which + half)
                pe.wait_ge(N["dve_oT"], 1 + NB - 1 if first else 1 + NB)
                pe.wait_ge(N["dve_oT2"], 1 + HB * j - (1 if which == 0 and not first else 0))
                for i in range(2):
                    for t in range(TOK):
                        h = 2 * half + i
                        last = nc.tensor.transpose(B[0][:, i * SEQ + t * P:i * SEQ + (t + 1) * P],
                                                   hraw[:, t, h * P:(h + 1) * P], ident)
                last.then_inc(N["pe_qkT"], 1)

            def da_mix(j, s, turning):
                for h, s0 in enumerate(HEAD_SLOTS):
                    if s == s0:
                        pe.wait_ge(N["act_qkT"], 1 + 4 * j + 4)
                        pe.wait_ge(N["dve_s1"], 1 + HB * j + h)
                        pe.wait_ge(N["dve_o2"], 1 + 2 * NB)
                        for t in range(TOK):
                            for m in range(2):
                                a = slice(m * CH, (m + 1) * CH)
                                last = mm(B[1 + m][:, t * P:t * P + (t + 1) * P],
                                          qT[a, h, t * P:(t + 1) * P], kT[a, h, 0:(t + 1) * P])
                        last.then_inc(N["pe_s"], 1)
                    if s == s0 + 4:
                        pe.wait_ge(N["dve_pd"], 1 + HB * j + h + 1)
                        pe.wait_ge(N["dve_oh2"], 1 + HB * j + h)
                        pe.wait_ge(N["dve_oT0"], 1 + NB)
                        for i in range(3):
                            last = nc.tensor.transpose(B[3][:, i * P:(i + 1) * P], pr[:, 0, i * P:(i + 1) * P], ident)
                        last.then_inc(N["pe_pT"], 1)
                    if s == s0 + 5:
                        pe.wait_ge(N["act_pT"], 1 + HB * j + h + 1)
                        mm(B[3][:, 0:P], pT[:, 0:P], vda[:, 0, h * P:(h + 1) * P])
                        mm(B[3][:, P:2 * P], pT[:, P:2 * P], vda[:, 0, h * P:(h + 1) * P], True, False)
                        mm(B[3][:, P:2 * P], pT[:, 2 * P:3 * P], vda[:, 1, h * P:(h + 1) * P], False, True
                           ).then_inc(N["pe_pv"], 1)
                    if s == s0 + 7:
                        if h == HB - 1 and turning:
                            pe.wait_ge(N["act_qkT"], 1 + 4 * (j + 1) + 2)
                        pe.wait_ge(N["dve_oh2"], 1 + HB * j + h + 1)
                        pe.wait_ge(N["dve_oT2"], 1 + HB * j + h)
                        pe.wait_ge(N["dve_oT"], 1 + NB)
                        for t in range(TOK):
                            last = nc.tensor.transpose(B[0][:, t * P:(t + 1) * P], oh[:, t, :], ident)
                        last.then_inc(N["pe_oT2"], 1)

            def turn_rows(cnt):
                pe.wait_ge(N["dve_m"], 1 + cnt + 1)
                pe.wait_ge(N["dve_mT"], 1 + cnt)
                for t in range(TOK):
                    for i in range(4):
                        last = nc.tensor.transpose(B4[t][:, i, :], hraw[:, t, i * P:(i + 1) * P], ident)
                last.then_inc(N["pe_mT"], 1)

            def body(n, g, a, mixes=(), before=None):
                for i in range(4):
                    pair = i % 2
                    pe.wait_ge(evac[pair], g + i // 2)
                    for q in range(TPG):
                        s = i * TPG + q
                        if before:
                            before(s)
                        gemm_tile(n + s, s, a, TK * q, pair, q == TPG - 1)
                        for mix in mixes:
                            mix(s)

            body(0, 0, act_x, [prologue, lambda s: dn_conv(0, s)], x_ready)
            pe.wait_ge(N["act_tot"], 1)
            with pe.Fori(1, NB) as j:
                body(j * BODY, 2 * j, act_x, [lambda s: dn_mix(j - 1, s), lambda s: dn_conv(j, s)])

            def da_turns(j, s, first):
                for which, slots in enumerate(DA_TURN_FIRST if first else DA_TURN):
                    if s in slots:
                        g = which if first else which + 1
                        da_turn(j, which, slots.index(s), (g % 2, 2 * NB + 2 * j + g // 2 + 1), first)

            body(N_DA, 2 * NB, act_x, [lambda s: dn_mix(NB - 1, s), lambda s: da_turns(0, s, True)])
            with pe.Fori(1, NB) as j:
                body(N_DA + j * BODY, 2 * NB + 2 * j, act_x,
                     [lambda s: da_mix(j - 1, s, True), lambda s: da_turns(j, s, False)])
            body(N_GB, 4 * NB, act_x, [lambda s: da_mix(NB - 1, s, False)])

            def pair_of_groups(n, g, regs, after, x1=False):
                for i in range(2):
                    pe.wait_ge(evac[i], g)
                    for q in range(TPG):
                        if x1 and i == 0:
                            if q == 0:
                                turn_x1(0)
                            if q % 2 == 0:
                                pe.wait_ge(N["dve_x1T"], q + 2)
                            elif q < TPG - 1:
                                turn_x1(q // 2 + 1)
                        gemm_tile(n + i * TPG + q, q, regs[i], TK * q, i, q == TPG - 1)
                        if i == 0 and q == 1 and after:
                            after()

            pe.wait_ge(N["dve_oT2"], 1 + HEADS)
            g0 = 4 * NB + 2
            pair_of_groups(N_BR, g0, (act_a, act_b), None)
            with pe.Fori(1, NB) as j:
                pair_of_groups(N_BR + 2 * TPG * j, g0 + j, (act_a, act_b), lambda: turn_rows(j - 1))

            def merged_ready(s):
                if s in (0, TPG - 2):
                    pe.wait_ge(N["dve_mT"], 1 + NB - (s == 0))
            body(N_OUT, g0 + NB, act_x, [lambda s: turn_rows(NB - 1) if s == 1 else None], merged_ready)

            def turn_x1(cq):
                for t in range(TOK):
                    i = TOK * cq + t
                    pe.wait_ge(N["dve_x1"], i + 1)
                    if i >= 4:
                        pe.wait_ge(N["dve_x1T"], i - 3)
                    for q in range(4):
                        last = nc.tensor.transpose(B4[i % 4][:, q, :],
                                                   y[:, t, (4 * cq + q) * P:(4 * cq + q + 1) * P], ident)
                    last.then_inc(N["pe_x1T"], 1)

            def up(n, g, cnt, place):
                pair_of_groups(n, g, (act_a, act_a), (lambda: turn_rows(cnt - 1)) if place else None,
                               isinstance(n, int) and n == N_FFN)

            def down(piece, n, g, tiles, buf, cnt, place):
                pe.wait_ge(N["dve_mT"], 1 + cnt - 1)
                for i in range(4):
                    pe.wait_ge(evac[i % 2], g + i // 2)
                    for q in range(tiles):
                        if piece == 2 and i == 0 and q == tiles - 2:
                            pe.wait_ge(N["dve_mT"], 1 + cnt)
                        gemm_tile(n + tiles * i + q, tiles * i + q, buf, TK * q, i % 2, q == tiles - 1)
                        if i == 0 and q == 1:
                            turn_rows(cnt - 1)
            ffn_walk(pe, up, down)


        @block.scalar
        def _(act):
            def copy(o, i, scale=1.0):
                return nc.scalar.activation(o, i, ACT.Copy, scale=scale)

            def split(n, s):
                if isinstance(n, int) and n + s + AHEAD >= N_TILES:
                    return
                rounds, r = divmod(s + AHEAD, RING)
                act.wait_ge(raw_full[r], (16 // RING) * n + 16 * (rounds + 1))
                act.wait_ge(tile_used, n + s)
                copy(whi[:, r], raw[:, r]).then_inc(hi_done, 1)

            for i in range(4):
                act.wait_ge(xt_full[i], 16)
                copy(act_x[:, 0, 4 * i:4 * i + 4, :], xt4[i]).then_inc(x_hi, 1)
                if i < AHEAD:
                    act.wait_ge(raw_full[i], 16)
                    copy(whi[:, i], raw[:, i]).then_inc(hi_done, 1)

            def prologue(s):
                if s == 2:
                    act.wait_ge(const_full, 80)
                    act.wait_ge(N["pe_ab"], 1)
                    for t in range(TOK):
                        nc.scalar.activation(scal[:, :, 4 * t:4 * t + 4],
                                             B[t][:, 0:HEADS].rearrange("p (j h) -> p j h", h=HB), ACT.Sigmoid
                                             ).then_inc(N["act_lam"], 1)
                    act.wait_ge(N["dve_lam"], 1)
                    nc.scalar.activation(lam[:, :], lam[:, :], ACT.Exp).then_inc(N["act_lam"], 1)
                    act.wait_ge(N["dve_sc0"], 1)
                    nc.scalar.activation(pz[:, 1, :], pz[:, 1, :], ACT.Exp, scale=-1.0)
                    nc.scalar.activation(pz[:, 3, 0:HEADS], par[:, slice(*PARAM["alog"])], ACT.Exp
                                         ).then_inc(N["act_pro"], 1)
                    act.wait_ge(x_lo, 4)
                if s == 6:
                    act.wait_ge(N["pe_sc0"], 1)
                    for t in range(TOK):
                        for f, at in (("eg", 0), ("tail", 32)):
                            a0 = SC[f][0] + 4 * t
                            nc.scalar.activation(scal[:, :, a0:a0 + 4],
                                                 B[2][:, at + HEADS * t:at + HEADS * t + HEADS]
                                                 .rearrange("p (j h) -> p j h", h=HB), ACT.Exp)
                        for p in range(2):
                            a0 = SC["total"][0] + 8 * t + 4 * p
                            at = 64 + 32 * p + HEADS * t
                            last = nc.scalar.activation(scal[:, :, a0:a0 + 4], B[2][:, at:at + HEADS].rearrange(
                                "p (j h) -> p j h", h=HB), ACT.Exp)
                    last.then_inc(N["act_tot"], 1)

            def rows_out(pair, dst, func=ACT.Copy):
                for t in range(TOK):
                    last = nc.scalar.activation(dst(t), pg[pair][t][:, :], func)
                last.then_inc(evac[pair], 1)

            def dn_evac(n, i, j):
                act.wait_ge(tile_used, n)
                if i < 3:
                    act.wait_ge(N["pe_conv"], 1 + 6 * j + 2 * i)
                    rows_out(i % 2, lambda t: hraw[:, t, :])
                else:
                    act.wait_ge(N["dve_oh"], 1 + 2 * j)
                    rows_out(1, lambda t: zs[:, t, :], ACT.Silu)

            def dn_conv(j, s):
                for kind, slots in enumerate(CONV_SLOTS):
                    if s in slots:
                        half = slots.index(s)
                        act.wait_ge(N["pe_conv"], 1 + 6 * j + 2 * kind + half + 1)
                        if half == 0:
                            act.wait_ge(N[("pe_ktok", "pe_v", "pe_a")[kind]], 1 + (1, 2, 3)[kind] * j)
                            act.wait_ge(N["dve_cw"], 1 + j + 1)
                        for i in range(2):
                            h = 2 * half + i
                            last = nc.scalar.activation(cT[:, kind, h, :], B[0][:, i * SEQ:(i + 1) * SEQ], ACT.Copy,
                                                        scale=cw[:, kind, h, CONV - 1:CONV])
                        last.then_inc(N["act_tap"], 1)
                    if s == slots[1] + 1:
                        act.wait_ge(N["dve_conv"], 1 + 6 * j + 2 * kind + 2)
                        nc.scalar.activation(cT[:, kind], cT[:, kind], ACT.Silu).then_inc(N["act_silu"], 1)

            def dn_mix(j, s):
                if s == 0:
                    act.wait_ge(N["pe_a"], 1 + 3 * j)
                    act.wait_ge(N["act_silu"], 1 + 3 * j + 3)
                    nc.scalar.activation(w_sq[:, :], cT[:, 2].rearrange("p h s -> p (h s)"), ACT.Square
                                         ).then_inc(N["act_sqq"], 1)
                    act.wait_ge(N["pe_ktok"], 1 + j + 1)
                    act.wait_ge(N["dve_vn"], 1 + 3 * j)
                    act.wait_ge(N["pe_b"], 1 + 4 * j)
                    for t in range(TOK):
                        last = nc.scalar.activation(u_sq[:, t], B4[1 + t], ACT.Square)
                    last.then_inc(N["act_sqk"], 1)
                if s == 1:
                    act.wait_ge(N["pe_dt"], 1 + j + 1)
                    act.wait_ge(N["dve_at"], 1 + j)
                    nc.scalar.activation(decm[:, :, :], B8[3], ACT.Exp).then_inc(N["act_decay"], 1)
                if s in (3, 4):
                    t = s - 3
                    act.wait_ge(N["pe_v"], 1 + 2 * j + t + 1)
                    act.wait_ge(N["pe_u"], 1 + j)
                    copy(vtok[:, t], B4[3]).then_inc(N["act_v"], 1)
                if s == 3:
                    act.wait_ge(N["pe_knT"], 1 + j + 1)
                    act.wait_ge(N["pe_oT"], 1 + 2 * j)
                    for t in range(TOK):
                        last = copy(knT_o[:, t], B4[1 + t])
                    last.then_inc(N["act_knT"], 1)
                if s == 6:
                    act.wait_ge(N["pe_br"], 1 + j + 1)
                    act.wait_ge(N["pe_w"], 1 + 2 * j)
                    copy(TTg[:, :, :], B8[3]).then_inc(N["act_br"], 1)
                if s == 18:
                    act.wait_ge(N["pe_u"], 1 + j + 1)
                    act.wait_ge(N["dve_kn"], 1 + j + 1)
                    for t in range(TOK):
                        last = copy(u_sq[:, t], B4[1 + t])
                    last.then_inc(N["act_u"], 1)
                if s in (18, 19):
                    p = s - 18
                    act.wait_ge(N["pe_w"], 1 + 2 * j + p + 1)
                    c0 = (1 - p) * NG // 2
                    copy(w_sq[:, p * NG + c0:(p + 1) * NG], B[3][:, c0:]).then_inc(N["act_w"], 1)
                if s in (CK_SLOTS[1] + 2, CK_SLOTS[3] + 2):
                    t = (s - CK_SLOTS[1]) // 5
                    act.wait_ge(N["dve_o2"], 1 + 2 * j + t + 1)
                    nc.scalar.activation(kn[:, t], knT_o[:, t], ACT.Square).then_inc(N["act_osq"], 1)
                if s == 31:
                    for t in range(TOK):
                        act.wait_ge(N["pe_oT"], 1 + 2 * j + t + 1)
                        copy(hi(act_a, HB * j, HB, t * P, (t + 1) * P), B4[3 - 3 * t]).then_inc(N["act_oT"], 1)

            def body(n, evac_fn, mixes=()):
                for s in range(BODY):
                    split(n, s)
                    for mix in mixes:
                        mix(s)
                    if s % TPG == TPG - 1:
                        evac_fn(n + s + 1, s // TPG)

            body(0, lambda n, i: dn_evac(n, i, 0), [prologue, lambda s: dn_conv(0, s)])
            with act.Fori(1, NB) as j:
                body(BODY * j, lambda n, i: dn_evac(n, i, j), [lambda s: dn_mix(j - 1, s), lambda s: dn_conv(j, s)])

            def da_evac(n, i, j, first):
                act.wait_ge(tile_used, n)
                what = ("q", "k", "v", "g")[i] if first else ("g", "q", "k", "v")[i]
                if what == "q":
                    act.wait_ge(N["pe_conv"], 1 + 6 * NB)
                    act.wait_ge(N["pe_qkT"], 1 + 4 * j)
                    rows_out(i % 2, lambda t: hraw[:, t, :])
                if what == "k":
                    act.wait_ge(N["pe_qkT"], 1 + 4 * j + 2)
                    rows_out(i % 2, lambda t: hraw[:, t, :])
                if what == "v":
                    act.wait_ge(N["pe_pv"], 1 + HB * j)
                    rows_out(i % 2, lambda t: vda[:, t, :])
                if what == "g":
                    act.wait_ge(N["dve_oT"], 1 + NB)
                    rows_out(i % 2, lambda t: gates[:, 0, t, bass.ds(NG * j, NG)], ACT.Sigmoid)

            def da_turns(j, s, first):
                for which, slots in enumerate(DA_TURN_FIRST if first else DA_TURN):
                    if s in slots:
                        half = slots.index(s)
                        act.wait_ge(N["pe_qkT"], 1 + 4 * j + 2 * which + half + 1)
                        act.wait_ge(N["pe_s"], 1 + HB * j)
                        copy((qT, kT)[which][:, 2 * half:2 * half + 2, :],
                             B[0][:, :].rearrange("p (h s) -> p h s", h=2), CH ** -0.5 if which == 0 else 1.0
                             ).then_inc(N["act_qkT"], 1)

            def da_mix(j, s):
                for h, s0 in enumerate(HEAD_SLOTS):
                    if s == s0 + 1:
                        act.wait_ge(N["dve_mx"], 1 + HB * j + h + 1)
                        for r, (a, b) in enumerate([(0, P), (P, 3 * P)]):
                            for m in range(2):
                                i = 2 * r + m
                                last = nc.scalar.activation(pr[:, m, a:b], pr[:, m, a:b], ACT.Exp,
                                                            bias=sm[:, 28 + i:29 + i], accum_out=sm[:, 32 + i:33 + i])
                        last.then_inc(N["act_exp"], 1)
                for h, s0 in enumerate(HEAD_SLOTS):
                    if s == s0 + 4:
                        act.wait_ge(N["pe_pT"], 1 + HB * j + h + 1)
                        act.wait_ge(N["pe_pv"], 1 + HB * j + h)
                        copy(pT[:, :], B[3][:, 0:3 * P]).then_inc(N["act_pT"], 1)
                    if s == s0 + 5:
                        act.wait_ge(N["pe_pv"], 1 + HB * j + h + 1)
                        for t in range(TOK):
                            last = nc.scalar.activation(pr[:, 1, t * P:(t + 1) * P], B[3][:, t * P:(t + 1) * P],
                                                        ACT.Square, accum_out=sm[:, 40 + t:41 + t])
                        last.then_inc(N["act_oss"], 1)
                    if s == s0 + 7:
                        act.wait_ge(N["pe_oT2"], 1 + HB * j + h + 1)
                        copy(hi(act_b, HB * j + h, 1), B[0][:, 0:SEQ].unsqueeze(1)).then_inc(N["act_oT2"], 1)

            body(N_DA, lambda n, i: da_evac(n, i, 0, True),
                 [lambda s: dn_mix(NB - 1, s), lambda s: da_turns(0, s, True)])
            with act.Fori(1, NB) as j:
                body(N_DA + BODY * j, lambda n, i: da_evac(n, i, j, False),
                     [lambda s: da_mix(j - 1, s), lambda s: da_turns(j, s, False)])

            def gb_evac(n, i):
                act.wait_ge(tile_used, n)
                rows_out(i % 2, lambda t: gates[:, 1, t, NG * i:NG * i + NG], ACT.Sigmoid)
            body(N_GB, gb_evac, [lambda s: da_mix(NB - 1, s)])

            def turn_rows(cnt, place):
                buf, k = place
                act.wait_ge(N["pe_mT"], 1 + cnt + 1)
                for t in range(TOK):
                    copy(hi(buf, k, 4, t * P, (t + 1) * P), B4[t]).then_inc(N["act_mT"], 1)

            def pair_of_groups(n, after):
                for s in range(2 * TPG):
                    split(n, s)
                    if s == 1 and after:
                        after()

            pair_of_groups(N_BR, None)
            with act.Fori(1, NB) as j:
                pair_of_groups(N_BR + 2 * TPG * j, lambda: turn_rows(j - 1, (act_x, 4 * (j - 1))))
            for s in range(BODY):
                split(N_OUT, s)
                if s == 1:
                    turn_rows(NB - 1, (act_x, 4 * (NB - 1)))

            def normalize(i, cq):
                for t in range(TOK):
                    act.wait_ge(N["act_var"], i + 1)
                    yv = y[:, t, cq * NG:(cq + 1) * NG]
                    nc.scalar.activation(yv, yv, ACT.Identity, bias=sm[:, 60 + t:61 + t], scale=sm[:, 58 + t:59 + t]
                                         ).then_inc(N["act_xn"], 1)

            def split_x1(cq):
                for t in range(TOK):
                    i = TOK * cq + t
                    act.wait_ge(N["pe_x1T"], i + 1)
                    copy(act_a[:, 0, 4 * cq:4 * cq + 4, t * P:(t + 1) * P], B4[i % 4]).then_inc(N["act_x1T"], 1)

            def up(n, g, cnt, place):
                first = isinstance(n, int) and n == N_FFN
                if first:
                    normalize(0, 0)
                    normalize(0, 1)
                    split_x1(0)
                for s in range(2 * TPG):
                    split(n, s)
                    if first and s in (0, 2, 4):
                        if s < 4:
                            normalize(0, s // 2 + 2)
                        split_x1(s // 2 + 1)
                    if s == 1 and place:
                        turn_rows(cnt - 1, place)
                    if s == TPG - 1:
                        act.wait_ge(tile_used, n + TPG)
                        act.wait_ge(N["dve_m"], 1 + cnt)
                        for t in range(TOK):
                            last = nc.scalar.activation(vda[:, t, :], pg[0][t][:, :], ACT.Silu)
                        last.then_inc(evac[0], 1)

            def down(piece, n, g, tiles, buf, cnt, place):
                for s in range(4 * tiles):
                    split(n, s)
                    if s == 1:
                        turn_rows(cnt - 1, place)

            ffn_walk(act, up, down)
            for cq in range(4):
                normalize(1, cq)

        @block.vector
        def _(dve):
            V = nc.vector

            def tt(o, a, b, op):
                return V.tensor_tensor(o, a, b, op)

            def ts(o, a, s1, op0, s2=None, op1=None):
                if op1 is None:
                    return V.tensor_scalar(o, a, s1, None, op0)
                return V.tensor_scalar(o, a, s1, s2, op0, op1)

            def stt(o, a, s, b, op0, op1):
                return V.scalar_tensor_tensor(out=o, in0=a, scalar=s, in1=b, op0=op0, op1=op1)

            def rsqrt(ch, o, x):
                a = sm[:, 64:64 + x.shape[1]]
                ch(V.tensor_single_scalar(o.bitcast(I32), x.bitcast(I32), 1, ALU.logical_shift_right))
                ch(ts(o.bitcast(I32), o.bitcast(I32), -1.0, ALU.mult, float(0x5F3759DF), ALU.add))
                for _ in range(3):
                    ch(stt(a, o, -0.5, o, ALU.mult, ALU.mult))
                    ch(tt(a, a, x, ALU.mult))
                    ch(stt(o, a, 1.5, o, ALU.add, ALU.mult))

            def split(n, s):
                if isinstance(n, int) and n + s + AHEAD >= N_TILES:
                    return
                r = (s + AHEAD) % RING
                dve.wait_ge(hi_done, n + s + AHEAD + 1)
                dve.wait_ge(tile_used, n + s)
                tt(wlo[:, r], raw[:, r], whi[:, r], ALU.subtract).then_inc(lo_done, 1)

            pro = Chain(dve, N["pro_chain"])
            for i in range(4):
                dve.wait_ge(x_hi, i + 1)
                tt(act_x[:, 1, 4 * i:4 * i + 4, :], xt4[i], act_x[:, 0, 4 * i:4 * i + 4, :], ALU.subtract
                   ).then_inc(x_lo, 1)
                if i < AHEAD:
                    dve.wait_ge(hi_done, i + 1)
                    tt(wlo[:, i], raw[:, i], whi[:, i], ALU.subtract).then_inc(lo_done, 1)

            def prologue(s):
                if s == 2:
                    dve.wait_ge(const_full, 80)
                    lv = vda[:, 0, 0:4 * CH].rearrange("p (a b d) -> p a b d", a=2, b=2)
                    pro(tt(vda[:, 1, 0:2 * CH].rearrange("p (a d) -> p a d", a=2), lv[:, :, 0, :], lv[:, :, 1, :], ALU.mult))
                    V.tensor_reduce(lam[:, :], vda[:, 1, 0:2 * CH].rearrange("p (a d) -> p a d", a=2), X, ALU.add
                                    ).then_inc(N["dve_lam"], 1)
                    dve.wait_ge(N["pe_ab"], 1)
                    dve.wait_ge(N["act_lam"], 2)
                    for t in range(TOK):
                        pro(tt(pz[:, 0, t * HEADS:(t + 1) * HEADS], B[t][:, HEADS:2 * HEADS], par[:, slice(*PARAM["dt"])],
                               ALU.add))
                    stt(pz[:, 1, :], pz[:, 0, :], -1.0, pz[:, 0, :], ALU.mult, ALU.max).then_inc(N["dve_sc0"], 1)
                if s == 3:
                    dve.wait_ge(N["act_pro"], 1)
                    e, r, r2 = pz[:, 1, :], pz[:, 2, :], g_all[:, :]
                    pro(ts(r, e, 2.0, ALU.add))
                    pro(V.reciprocal(r, r))
                    pro(tt(r, r, e, ALU.mult))
                    pro(tt(r2, r, r, ALU.mult))
                    pro(ts(e, r2, 2.0 / 17, ALU.mult, 2.0 / 15, ALU.add))
                    for k in range(6, -1, -1):
                        pro(tt(e, e, r2, ALU.mult))
                        pro(ts(e, e, 2.0 / (2 * k + 1), ALU.add))
                    pro(tt(e, e, r, ALU.mult))
                    pro(stt(e, pz[:, 0, :], 0.0, e, ALU.max, ALU.add))
                    for t in range(TOK):
                        a = slice(t * HEADS, (t + 1) * HEADS)
                        pro(stt(g_all[:, a], e[:, a], -1.0, pz[:, 3, 0:HEADS], ALU.mult, ALU.mult))
                        g0 = SC["g"][0] + 4 * t
                        pro(V.tensor_copy(scal[:, :, g0:g0 + 4], g_all[:, a].rearrange("p (j h) -> p j h", h=HB)))
                    dve.wait_ge(N["act_lam"], 3)
                    ts(lam[:, 0:1], lam[:, 0:1], lam[:, 1:2], ALU.subtract, LAMBDA_INIT, ALU.add).then_inc(N["dve_pro"], 1)

            def dn_conv(j, s):
                if s == 4:
                    dve.wait_ge(N["act_tap"], 1 + 6 * j)
                    a0 = PARAM["conv"][0]
                    V.tensor_copy(cw[:, :, :, :].rearrange("p k h c -> p (k h c)").unsqueeze(1),
                                  par[:, a0:a0 + NB * 48].rearrange("p (j c) -> p j c", j=NB)
                                  [:, bass.ds(j, 1), :]).then_inc(N["dve_cw"], 1)
                for kind, slots in enumerate(CONV_SLOTS):
                    if s not in slots:
                        continue
                    half = slots.index(s)
                    link = Chain(dve, N["conv_chain"], 1 + CONV_LINKS * j + 2 * (2 * kind + half))
                    dve.wait_ge(N["act_tap"], 1 + 6 * j + 2 * kind + half + 1)
                    for back in range(1, CONV):
                        for i in range(2):
                            h = 2 * half + i
                            w = cw[:, kind, h, CONV - 1 - back:CONV - back]
                            dst = cT[:, kind, h, back:SEQ]
                            ins = stt(dst, B[0][:, i * SEQ:(i + 1) * SEQ - back], w, dst, ALU.mult, ALU.add)
                        if back == CONV - 1:
                            ins.then_inc(N["dve_conv"], 1)
                        else:
                            link(ins)

            def dn_mix(j, s, ch):
                if s == 0:
                    dve.wait_ge(N["pe_t"], 1 + (LEVELS - 1) * j)
                    dve.wait_ge(N["pe_u"], 1 + j)
                    ch(V.tensor_copy(cur[:, :].unsqueeze(1), scal[:, bass.ds(j, 1), :]))
                    tt(Pm[:, :, :], rep(c("upto"), 8), bc(s_("g"), CH), ALU.mult)
                    tt(TTb[:, :, :], rep(c("eye"), 8), bc(s_("beta"), CH), ALU.mult).then_inc(N["dve_rows"], 1)
                    ch(tt(sm[:, 16:24], s_("beta"), s_("eg"), ALU.mult))
                if s == 1:
                    dve.wait_ge(N["act_sqk"], 1 + j + 1)
                    dve.wait_ge(N["pe_w"], 1 + 2 * j)
                    ch(V.tensor_reduce(sm[:, 0:8], u8, X, ALU.add))
                    ch(ts(sm[:, 0:8], sm[:, 0:8], RMS_EPS, ALU.add))
                    rsqrt(ch, sm[:, 48:56], sm[:, 0:8])
                    for t in range(TOK):
                        last = tt(kn[:, t], B4[1 + t], bc(sm[:, 48 + 4 * t:52 + 4 * t], P), ALU.mult)
                    last.then_inc(N["dve_kn"], 1)
                if s == 4:
                    dve.wait_ge(N["dve_kn"], 1 + j + 1)
                    dve.wait_ge(N["pe_b"], 1 + 4 * j)
                    ch(tt(ktail8, kn8, bc(s_("tail"), P), ALU.mult))
                if s == 2:
                    dve.wait_ge(N["pe_qss"], 1 + j + 1)
                    ts(sm[:, 56:64], B[3][:, 0:8], RMS_EPS, ALU.add, float(P), ALU.mult).then_inc(N["dve_rq"], 1)
                    dve.wait_ge(N["act_decay"], 1 + j + 1)
                    ch(tt(decm[:, :, :], decm[:, :, :], rep(c("incl"), 8), ALU.mult))
                if s == 3:
                    dve.wait_ge(N["dve_rq"], 1 + j + 1)
                    rsqrt(ch, sm[:, 0:8], sm[:, 56:64])
                    ch(tt(sm[:, 8:16], sm[:, 0:8], sm[:, 0:8], ALU.mult))
                if s == 15:
                    dve.wait_ge(evac[1], 2 * j + 2)
                    ch(tt(zs8, zs8, rep(par[:, slice(*PARAM["dnw"])], 8), ALU.mult))
                if s == 5:
                    dve.wait_ge(N["pe_kq"], 1 + j + 1)
                    ch(tt(AT[:, :, :], B8[1], decm[:, :, :], ALU.mult))
                    ch(tt(QKT[:, :, :], B8[2], decm[:, :, :], ALU.mult))
                if s == 6:
                    dve.wait_ge(N["act_br"], 1 + j + 1)
                    tt(AT[:, :, :], AT[:, :, :], TTg[:, :, :], ALU.mult).then_inc(N["dve_at"], 1)
                    dve.wait_ge(N["dve_at"], 1 + j + 1)
                    ch(tt(TT[:, :, :], AT[:, :, :], rep(c("pairs"), 8), ALU.mult))
                    ch(tt(TT[:, :, :], rep(c("eye"), 8), TT[:, :, :], ALU.subtract))
                if s == 7:
                    dve.wait_ge(N["pe_p"], 1 + LEVELS * j + 1)
                    a0 = CONST["level"][0]
                    ch(tt(Pm[:, :, :], B8[1], rep(cst[:, a0:a0 + CH], 8), ALU.mult))
                    tt(T[:, :, :], rep(c("eye"), 8), Pm[:, :, :], ALU.subtract).then_inc(N["dve_t"], 1)
                if 8 <= s < 8 + 2 * (LEVELS - 1):
                    lv, odd = divmod(s - 6, 2)
                    a0 = CONST["level"][0] + lv * CH
                    if not odd:
                        dve.wait_ge(N["pe_p"], 1 + LEVELS * j + lv + 1)
                        tt(Pm[:, :, :], B8[1], rep(cst[:, a0:a0 + CH], 8), ALU.mult).then_inc(N["dve_p"], 1)
                    else:
                        dve.wait_ge(N["pe_t"], 1 + (LEVELS - 1) * j + lv)
                        ins = tt(TT[:, :, :], TT[:, :, :], B8[2], ALU.subtract)
                        if lv < LEVELS - 1:
                            ins = tt(T[:, :, :], T[:, :, :], B8[3], ALU.subtract)
                        ins.then_inc(N["dve_t"], 1)
                if s == 17:
                    dve.wait_ge(N["dve_t"], 1 + LEVELS * (j + 1))
                    tt(TTb[:, :, :], TT[:, :, :], bc(s_("beta"), CH), ALU.mult)
                    tt(TTg[:, :, :], TT[:, :, :], bc(sm[:, 16:24], CH), ALU.mult).then_inc(N["dve_tb"], 1)
                if s == 18:
                    ch(V.memset(knT_o[0:CH, 0], 0.0))
                for ck in range(4):
                    t, p = divmod(ck, 2)
                    a = slice(p * CH, (p + 1) * CH)
                    if s == CK_SLOTS[ck] and ck:
                        dve.wait_ge(N["pe_a"], 1 + 3 * j + ck)
                        dve.wait_ge(N["act_u"], 1 + j + 1)
                        tt(vn[a], u_sq[a, t], B4[1][a], ALU.subtract).then_inc(N["dve_vn"], 1)
                        if ck < 3:
                            t0 = SC["total"][0] + 4 * ck
                            ch(tt(S[:, :, :], S[:, :, :], bc(cur[:, t0:t0 + 4], P), ALU.mult))
                    if s == CK_SLOTS[ck] + 1:
                        dve.wait_ge(N["pe_b"], 1 + 4 * j + ck + 1)
                        if ck == 0:
                            V.tensor_copy(S[:, :, :], B4[1]).then_inc(N["dve_s"], 1)
                            dve.wait_ge(N["dve_s"], 1 + 3 * j + 1)
                        elif ck < 3:
                            tt(S[:, :, :], S[:, :, :], B4[1], ALU.add).then_inc(N["dve_s"], 1)
                        if p:
                            e0 = SC["eg"][0] + 4 * t
                            rows = slice(CH if ck == 1 else 0, P)
                            eg = cur[rows, e0:e0 + 4].unsqueeze(2).broadcast_to([P - rows.start, 4, P])
                            tt(knT_o[rows, t], B4[2][rows], eg, ALU.mult).then_inc(N["dve_o1"], 1)
                            dve.wait_ge(N["dve_o1"], 1 + 2 * j + t + 1)
                            tt(knT_o[:, t], knT_o[:, t], B4[3], ALU.add).then_inc(N["dve_o2"], 1)
                if s in (24, 28):
                    t = (s - 24) // 4
                    dve.wait_ge(N["act_osq"], 1 + 2 * j + t + 1)
                    ch(V.tensor_reduce(sm[:, 24 + 4 * t:28 + 4 * t], kn[:, t], X, ALU.add))
                if s == 28:
                    ch(stt(sm[:, 24:32], sm[:, 24:32], 1.0 / P, sm[:, 8:16], ALU.mult, ALU.mult))
                    ch(ts(sm[:, 24:32], sm[:, 24:32], RMS_EPS, ALU.add))
                    rsqrt(ch, sm[:, 48:56], sm[:, 24:32])
                    ch(tt(sm[:, 24:32], sm[:, 48:56], sm[:, 0:8], ALU.mult))
                    for t in range(TOK):
                        ch(tt(knT_o[:, t], knT_o[:, t], bc(sm[:, 24 + 4 * t:28 + 4 * t], P), ALU.mult))
                        tt(knT_o[:, t], knT_o[:, t], zs[:, t, :].rearrange("p (h d) -> p h d", h=HB), ALU.mult
                           ).then_inc(N["dve_oh"], 1)
                if s == 31:
                    for t in range(TOK):
                        dve.wait_ge(N["act_oT"], 1 + 2 * j + t + 1)
                        tt(lo(act_a, HB * j, HB, t * P, (t + 1) * P), B4[3 - 3 * t],
                           hi(act_a, HB * j, HB, t * P, (t + 1) * P), ALU.subtract
                           ).then_inc(N["dve_oT" if t else "dve_oT0"], 1)

            def body(n, mixes=()):
                for s in range(BODY):
                    split(n, s)
                    for mix in mixes:
                        mix(s)

            def chained(name, base, fn, j, links, slots=BODY):
                ch = Chain(dve, N[name], 1 + base)
                def run(s):
                    fn(j, s, ch)
                    if s == slots - 1:
                        assert ch.n == links, (name, ch.n)
                return run

            body(0, [prologue, lambda s: dn_conv(0, s)])
            dve.wait_ge(N["act_tot"], 1)
            with dve.Fori(1, NB) as j:
                body(BODY * j, [chained("dn_chain", DN_LINKS * (j - 1), dn_mix, j - 1, DN_LINKS),
                                lambda s: dn_conv(j, s)])

            def da_mix(j, s, ch):
                if s == 0:
                    a0 = CONST["slopes"][0]
                    ch(V.tensor_copy(sm[:, 44:48].unsqueeze(1), cst[:, a0:a0 + HEADS].rearrange(
                        "p (j h) -> p j h", j=NB)[:, bass.ds(j, 1), :]))
                for h, s0 in enumerate(HEAD_SLOTS):
                    if s == s0:
                        dve.wait_ge(N["pe_s"], 1 + HB * j + h + 1)
                        dve.wait_ge(N["act_oss"], 1 + HB * j + h)
                        for m in range(2):
                            ins = stt(pr[:, m, :], c("negdist"), sm[:, 44 + h:45 + h], B[1 + m][:, 0:3 * P],
                                      ALU.mult, ALU.add)
                        ins.then_inc(N["dve_s1"], 1)
                        dve.wait_ge(N["dve_s1"], 1 + HB * j + h + 1)
                        V.tensor_reduce(sm[:, 24:26], pr[:, :, 0:P], X, ALU.max)
                        ch(V.tensor_reduce(sm[:, 26:28], pr[:, :, P:3 * P], X, ALU.max))
                        ts(sm[:, 28:32], sm[:, 24:28], -1.0, ALU.mult).then_inc(N["dve_mx"], 1)
                    if s == s0 + 2:
                        dve.wait_ge(N["act_exp"], 1 + HB * j + h + 1)
                        ch(V.reciprocal(sm[:, 36:40], sm[:, 32:36]))
                        ch(ts(sm[:, 37:40:2], sm[:, 37:40:2], lam[:, 0:1], ALU.mult))
                        for r, (a, b) in enumerate([(0, P), (P, 3 * P)]):
                            ins = ts(pr[:, 1, a:b], pr[:, 1, a:b], sm[:, 37 + 2 * r:38 + 2 * r], ALU.mult)
                        ch(ins)
                        for r, (a, b) in enumerate([(0, P), (P, 3 * P)]):
                            ins = stt(pr[:, 0, a:b], pr[:, 0, a:b], sm[:, 36 + 2 * r:37 + 2 * r], pr[:, 1, a:b],
                                      ALU.mult, ALU.subtract)
                        ins.then_inc(N["dve_pd"], 1)
                    if s == s0 + 5:
                        dve.wait_ge(N["act_oss"], 1 + HB * j + h + 1)
                        dve.wait_ge(N["pe_oT2"], 1 + HB * j + h)
                        ch(ts(sm[:, 42:44], sm[:, 40:42], 1.0 / P, ALU.mult, RMS_EPS, ALU.add))
                        rsqrt(ch, sm[:, 48:50], sm[:, 42:44])
                        ch(tt(oh[:, :, :], B[3][:, 0:SEQ].rearrange("p (t d) -> p t d", t=TOK), bc(sm[:, 48:50], P),
                              ALU.mult))
                        stt(oh[:, :, :], oh[:, :, :], 1.0 - LAMBDA_INIT, rep(par[:, slice(*PARAM["daw"])], TOK),
                            ALU.mult, ALU.mult).then_inc(N["dve_oh2"], 1)
                    if s == s0 + 7:
                        dve.wait_ge(N["act_oT2"], 1 + HB * j + h + 1)
                        tt(lo(act_b, HB * j + h, 1), B[0][:, 0:SEQ].unsqueeze(1), hi(act_b, HB * j + h, 1), ALU.subtract
                           ).then_inc(N["dve_oT2"], 1)

            body(N_DA, [chained("dn_chain", DN_LINKS * (NB - 1), dn_mix, NB - 1, DN_LINKS)])
            with dve.Fori(1, NB) as j:
                body(N_DA + BODY * j, [chained("da_chain", DA_LINKS * (j - 1), da_mix, j - 1, DA_LINKS)])
            body(N_GB, [chained("da_chain", DA_LINKS * (NB - 1), da_mix, NB - 1, DA_LINKS)])

            def turn_rows(cnt, place):
                buf, k = place
                for t in range(TOK):
                    dve.wait_ge(N["act_mT"], 1 + 2 * cnt + t + 1)
                    ins = tt(lo(buf, k, 4, t * P, (t + 1) * P), B4[t], hi(buf, k, 4, t * P, (t + 1) * P), ALU.subtract)
                ins.then_inc(N["dve_mT"], 1)

            def branch(n, j, turned):
                for s in range(2 * TPG):
                    split(n, s)
                    if s == 1 and turned:
                        turn_rows(j - 1, (act_x, 4 * (j - 1)))
                    if s == TPG - 1:
                        dve.wait_ge(tile_used, n + s + 1)
                        dve.wait_ge(N["pe_qkT"], 1 + 4 * NB)
                        dve.wait_ge(N["pe_mT"], 1 + j)
                        for t in range(TOK):
                            ins = tt(hraw[:, t, :], pg[0][t][:, :], gates[:, 0, t, bass.ds(NG * j, NG)], ALU.mult)
                        ins.then_inc(evac[0], 1)
                    if s == 2 * TPG - 1:
                        dve.wait_ge(tile_used, n + s + 1)
                        for t in range(TOK):
                            ins = tt(vda[:, t, :], pg[1][t][:, :], gates[:, 1, t, bass.ds(NG * j, NG)], ALU.mult)
                        ins.then_inc(evac[1], 1)
                        dve.wait_ge(evac[1], 4 * NB + 2 + j + 1)
                        tt(hraw[:, :, :], hraw[:, :, :], vda[:, :, :], ALU.add).then_inc(N["dve_m"], 1)

            branch(N_BR, 0, False)
            with dve.Fori(1, NB) as j:
                branch(N_BR + 2 * TPG * j, j, True)
            for g in range(4):
                for q in range(TPG):
                    split(N_OUT, g * TPG + q)
                    if g == 0 and q == 1:
                        turn_rows(NB - 1, (act_x, 4 * (NB - 1)))
                dve.wait_ge(tile_used, N_OUT + (g + 1) * TPG)
                dve.wait_ge(xres_full[g % 2], 16 * (g // 2 + 1))
                for t in range(TOK):
                    ins = stt(y[:, t, g * NG:(g + 1) * NG], xres[g % 2][:, t, :], ALPHA, pg[g % 2][t][:, :],
                              ALU.mult, ALU.add)
                ins.then_inc(evac[g % 2], 1)
                dve.wait_ge(evac[g % 2], 4 * NB + 2 + NB + g // 2 + 1)
                for t in range(TOK):
                    ins = V.bn_stats(lnst[:, t, g, :], y[:, t, g * NG:(g + 1) * NG])
                ins.then_inc(xres_used, 1)

            lnc = Chain(dve, N["ln_chain"])

            def moments():
                for t in range(TOK):
                    lnc(V.bn_aggr(lnmv[:, t, :], lnst[:, t, :, :].rearrange("p g s -> p (g s)")))
                lnc(ts(sm[:, 56:58], lnmv[:, :, 1], LN_EPS, ALU.add))
                rsqrt(lnc, sm[:, 58:60], sm[:, 56:58])
                stt(sm[:, 60:62], lnmv[:, :, 0], -1.0, sm[:, 58:60], ALU.mult, ALU.mult).then_inc(N["act_var"], 1)

            def gain(i, cq):
                a = slice(cq * NG, (cq + 1) * NG)
                for t in range(TOK):
                    dve.wait_ge(N["act_xn"], 8 * i + TOK * cq + t + 1)
                    lnc(tt(y[:, t, a], y[:, t, a], lnp[:, 0, a], ALU.mult))
                    tt(y[:, t, a], y[:, t, a], lnp[:, 1, a], ALU.add).then_inc(N["dve_x1"], 1)

            def split_x1(cq):
                for t in range(TOK):
                    i = TOK * cq + t
                    dve.wait_ge(N["act_x1T"], i + 1)
                    tt(act_a[:, 1, 4 * cq:4 * cq + 4, t * P:(t + 1) * P], B4[i % 4],
                       act_a[:, 0, 4 * cq:4 * cq + 4, t * P:(t + 1) * P], ALU.subtract).then_inc(N["dve_x1T"], 1)

            def up(n, g, cnt, place):
                first = isinstance(n, int) and n == N_FFN
                if first:
                    dve.wait_ge(xres_used, 4)
                    moments()
                    dve.wait_ge(ln_full, 64)
                    gain(0, 0)
                    split_x1(0)
                for s in range(2 * TPG):
                    split(n, s)
                    if first and s in (0, 2, 4):
                        gain(0, s // 2 + 1)
                    if first and s in (1, 3, 5):
                        split_x1((s + 1) // 2)
                    if s == 1 and place:
                        turn_rows(cnt - 1, place)
                dve.wait_ge(tile_used, n + 2 * TPG)
                dve.wait_ge(evac[0], g + 1)
                dve.wait_ge(N["pe_mT"], 1 + cnt)
                for t in range(TOK):
                    ins = tt(hraw[:, t, :], pg[1][t][:, :], vda[:, t, :], ALU.mult)
                ins.then_inc(N["dve_m"], 1)
                dve.wait_ge(N["dve_m"], 1 + cnt + 1)
                dve.sem_inc(evac[1], 1)

            def down_half(piece, n, g, i, tiles, cnt, place):
                for e in range(2):
                    for q in range(tiles):
                        split(n + 2 * tiles * i, e * tiles + q)
                        if i == e == 0 and q == 1:
                            turn_rows(cnt - 1, place)
                    dve.wait_ge(tile_used, n + 2 * tiles * i + (e + 1) * tiles)
                    for t in range(TOK):
                        yv = y[:, t, (2 * i + e) * NG:(2 * i + e + 1) * NG]
                        ins = stt(yv, yv, ALPHA if piece == 0 else 1.0, pg[e][t][:, :], ALU.mult, ALU.add)
                    ins.then_inc(evac[e], 1)
                    if piece == 2:
                        dve.wait_ge(evac[e], g + i + 1)
                        for t in range(TOK):
                            ins = V.bn_stats(lnst[:, t, 2 * i + e, :], y[:, t, (2 * i + e) * NG:(2 * i + e + 1) * NG])
                        lnc(ins)

            def down(piece, n, g, tiles, buf, cnt, place):
                for i in range(2):
                    down_half(piece, n, g, i, tiles, cnt, place)

            ffn_walk(dve, up, down)
            moments()
            dve.wait_ge(ln_full, 80)
            for cq in range(4):
                gain(1, cq)


def _constants():
    i = np.arange(P)
    same = (i[:, None] // CH == i[None, :] // CH)
    cc = np.arange(CH)
    ic = i % CH
    out = np.zeros((P, NCONST), np.float32)

    def put(name, a):
        out[:, slice(*CONST[name])] = a
    put("ident", np.eye(P))
    put("after", same & (i[:, None] > i[None, :]))
    put("same", same)
    put("upto", ic[:, None] <= cc[None, :])
    put("eye", ic[:, None] == cc[None, :])
    put("incl", cc[None, :] >= ic[:, None])
    lv = []
    for b in range(LEVELS):
        w = 1 << b
        lv.append((ic[:, None] // (2 * w) == cc[None, :] // (2 * w))
                  & (ic[:, None] // w % 2 == 1) & (cc[None, :] // w % 2 == 0))
    put("pairs", (ic[:, None] // 2 == cc[None, :] // 2) & (ic[:, None] % 2 == 0) & (cc[None, :] % 2 == 1))
    put("level", np.concatenate(lv, 1))
    d0 = (i[:, None] - i[None, :]).astype(np.float32)
    d1 = (P + i[:, None] - np.arange(SEQ)[None, :]).astype(np.float32)
    put("negdist", np.concatenate([np.where(d >= 0, -d, np.float32(-1e30)) for d in (d0, d1)], 1))
    put("slopes", np.broadcast_to(np.exp2(-8.0 * np.arange(1, HEADS + 1) / HEADS), (P, HEADS)))
    early = np.concatenate([same & (i[:, None] <= i[None, :]), np.broadcast_to(i[:, None] < CH, (P, P)),
                            np.broadcast_to(i[:, None] >= CH, (P, P))], 1).astype(np.float32)
    return out, early


def _tiles(w):
    k, n = w.shape
    return w.reshape(k // (TK * P), TK, P, n // NG, NG).transpose(3, 0, 2, 1, 4).reshape(n // NG, k // (TK * P), P, TK * NG)


def kernel(**inputs):
    import concourse.bacc as bacc
    from concourse.bass_utils import run_bass_kernel_spmd

    a = {k: np.asarray(v) for k, v in inputs.items()}
    x = a["x"][0]
    w = a["w_in"][0]
    qkv = HEADS * P
    at = {"q": 0, "k": qkv, "v": 2 * qkv, "z": 3 * qkv}
    ab = w[:, 4 * qkv:4 * qkv + 2 * HEADS]
    o = 4 * qkv + 2 * HEADS
    at.update({"aq": o, "ak": o + qkv, "av": o + 2 * qkv, "ga": o + 3 * qkv, "gb": o + 3 * qkv + D})
    order = [(n, j) for j in range(NB) for n in ("k", "v", "q", "z")]
    order += [(n, 0) for n in ("aq", "ak", "av", "ga")]
    order += [(n, j) for j in range(1, NB) for n in ("ga", "aq", "ak", "av")]
    order += [("gb", j) for j in range(NB)]
    stream = [_tiles(w[:, at[n] + NG * j:at[n] + NG * (j + 1)])[0] for n, j in order]
    wa, wb, wo = (_tiles(a[n][0]) for n in ("w_branch_a", "w_branch_b", "w_out"))
    for j in range(NB):
        stream += [wa[j], wb[j]]
    stream += [wo[j] for j in range(4)]
    wg, wu, wd = (_tiles(a[n][0]) for n in ("w_gate", "w_up", "w_down"))

    def ups(f0, f1):
        for f in range(f0, f1):
            stream.append(wg[f])
            stream.append(wu[f])

    def down(p):
        f0, f1 = PIECES[p]
        for g in range(4):
            stream.append(wd[g][2 * f0:2 * f1])
    ups(0, 5)
    down(0)
    ups(5, 9)
    down(1)
    ups(9, FG)
    down(2)
    weights = np.concatenate(stream, 0)
    consts, early = _constants()

    def wide(v):
        return np.broadcast_to(v.reshape(1, -1), (P, v.size))
    cv = a["conv_w"][0].reshape(CONV, 3, NB, HB, P)[:, [1, 2, 0]]
    params = np.concatenate([cv.transpose(4, 2, 1, 3, 0).reshape(P, -1), wide(a["dn_norm_w"][0]),
                             wide(a["da_norm_w"][0]), wide(a["dt_bias"][0]), wide(a["a_log"][0])], 1)
    ln_in = np.stack([np.broadcast_to(np.stack([a["ln_g"][0, i], a["ln_b"][0, i]]), (P, 2, D)) for i in range(2)])
    data = {
        "xT": x.T.reshape(4, 4, P, SEQ).transpose(0, 2, 1, 3),
        "xrow": x.reshape(TOK, P, 4, NG).transpose(2, 1, 0, 3),
        "weights": weights,
        "w_ab": ab.reshape(KC, P, 2 * HEADS).transpose(1, 0, 2).reshape(P, -1),
        "consts": consts, "early": early, "params": params, "lam_in": wide(a["da_lambda"][0]), "ln_in": ln_in,
    }
    nc = bacc.Bacc("TRN2", target_bir_lowering=False, num_devices=1)
    arrays, aps = {}, []
    for name, v in data.items():
        arrays["in_" + name] = np.ascontiguousarray(v)
        aps.append(nc.dram_tensor("in_" + name, v.shape, mybir.dt.from_np(v.dtype), kind="ExternalInput").ap())
    aps.append(nc.dram_tensor("out", (1, SEQ, D), F32, kind="ExternalOutput").ap())
    build(nc, *aps)
    r = run_bass_kernel_spmd(nc, [arrays], core_ids=[0])
    return r.results[0]["out"]
```
